# Optimizing a Trainium2 kernel written in Bass

```python
import jax, jax.numpy as jnp
from jax import lax
import numpy as np

D_MODEL = 1024
BATCH = 1
SEQ = 512
DEPTH = 1
DEC_BATCH = 8
DEC_SEQ = 1
PAST_LEN = 4096
PAGE_SIZE = 128

HEAD_DIM = 64
N_HEADS_TOTAL = D_MODEL // HEAD_DIM
N_ATT_HEADS = N_HEADS_TOTAL // 2
N_RWKV_HEADS = N_HEADS_TOTAL - N_ATT_HEADS
ATT_WIDTH = N_ATT_HEADS * HEAD_DIM
RWKV_WIDTH = N_RWKV_HEADS * HEAD_DIM
DIL_PATTERNS = ((128, 1), (512, 4), (2048, 16))
MAX_WIN = max(w for w, _ in DIL_PATTERNS)
Q_BLOCK = 128
DECAY_LORA = max(32, int(round(1.8 * D_MODEL ** 0.5 / 32.0)) * 32)
AAA_LORA = max(32, int(round(1.8 * D_MODEL ** 0.5 / 32.0)) * 32)
GATE_LORA = max(32, int(round(0.6 * D_MODEL ** 0.8 / 32.0)) * 32)
D_FF = 256 * int(round(8 * D_MODEL / 3 / 256))
CONV_W = 3
LN_EPS = 1e-5
GN_EPS = 64e-5
ALPHA = (2.0 * DEPTH) ** 0.25
BETA = (8.0 * DEPTH) ** -0.25
RW_SPLITS = (RWKV_WIDTH, 2 * RWKV_WIDTH, 3 * RWKV_WIDTH, 3 * RWKV_WIDTH + DECAY_LORA, 3 * RWKV_WIDTH + DECAY_LORA + AAA_LORA)
RW_COLS = 3 * RWKV_WIDTH + DECAY_LORA + AAA_LORA + GATE_LORA
IN_COLS = 3 * ATT_WIDTH + RW_COLS

kernel_name = 'hymba_dilated_alibi_rwkv7_convffn_deepnorm_step'

def layer_norm(x, g, b):
    xf = x.astype(jnp.float32)
    mu = jnp.mean(xf, -1, keepdims=True)
    xc = xf - mu
    var = jnp.mean(xc * xc, -1, keepdims=True)
    return (xc * lax.rsqrt(var + LN_EPS) * g + b).astype(x.dtype)

def alibi_slopes(n):
    return jnp.exp2(-8.0 * jnp.arange(1, n + 1, dtype=jnp.float32) / n)

def dilated_window_attention(q, k_all, v_all, prefix):
    B, T, H, Dh = q.shape
    slopes = alibi_slopes(H)
    scale = HEAD_DIM ** -0.5
    pad = ((0, 0), (MAX_WIN, 0), (0, 0), (0, 0))
    k_pad = jnp.pad(k_all, pad)
    v_pad = jnp.pad(v_all, pad)
    qb = Q_BLOCK if T % Q_BLOCK == 0 else T
    nb = T // qb
    q_blocks = q.reshape(B, nb, qb, H, Dh).transpose(1, 0, 2, 3, 4)
    starts = prefix + jnp.arange(nb, dtype=jnp.int32) * qb

    def one_block(args):
        q_blk, start = args
        pos = start + jnp.arange(qb, dtype=jnp.int32)
        lses, outs = [], []
        for win, dil in DIL_PATTERNS:
            dist = jnp.arange(win // dil + 1, dtype=jnp.int32) * dil
            idx = pos[:, None] - dist[None, :]
            kg = jnp.take(k_pad, idx + MAX_WIN, axis=1)
            vg = jnp.take(v_pad, idx + MAX_WIN, axis=1)
            s = jnp.einsum('bqhd,bqnhd->bhqn', q_blk, kg, preferred_element_type=jnp.float32) * scale
            s = s - slopes[:, None, None] * dist.astype(jnp.float32)
            s = jnp.where((idx >= 0)[None, None], s, -jnp.inf)
            lse = jax.nn.logsumexp(s, axis=-1)
            p = jnp.exp(s - lse[..., None])
            outs.append(jnp.einsum('bhqn,bqnhd->bqhd', p, vg.astype(jnp.float32)))
            lses.append(lse)
        lse_all = jnp.stack(lses)
        wts = jnp.exp(lse_all - jax.nn.logsumexp(lse_all, axis=0, keepdims=True))
        wts = jnp.transpose(wts, (0, 1, 3, 2))[..., None]
        return jnp.sum(wts * jnp.stack(outs), axis=0).astype(q.dtype)

    out = lax.map(one_block, (q_blocks, starts))
    return out.transpose(1, 0, 2, 3, 4).reshape(B, T, H, Dh)

def rwkv7_time_mix(rw, wkv0, w0, w_lora_up, a0, a_lora_up, g_lora_up, k_k, k_a, r_k, gn_w, gn_b):
    f32 = jnp.float32
    B, T, _ = rw.shape
    r, k, v, w_low, a_low, g_low = jnp.split(rw.astype(f32), RW_SPLITS, axis=-1)
    w_log = -jax.nn.softplus(-(w0 + jnp.tanh(w_low) @ w_lora_up)) - 0.5
    decay = jnp.exp(-jnp.exp(w_log))
    a = jax.nn.sigmoid(a0 + a_low @ a_lora_up)
    g = jax.nn.sigmoid(g_low) @ g_lora_up
    heads = lambda t: t.reshape(B, T, N_RWKV_HEADS, HEAD_DIM)
    kk = heads(k * k_k)
    kk = kk / jnp.maximum(jnp.linalg.norm(kk, axis=-1, keepdims=True), 1e-12)
    k = heads(k * (1.0 + (a - 1.0) * k_a))
    r, v, decay, a = heads(r), heads(v), heads(decay), heads(a)

    def step(S, inp):
        r_t, w_t, k_t, v_t, kk_t, a_t = inp
        sa = jnp.einsum('bhvk,bhk->bhv', S, -kk_t)
        S = S * w_t[:, :, None, :] + sa[..., None] * (kk_t * a_t)[:, :, None, :] + v_t[..., None] * k_t[:, :, None, :]
        return S, jnp.einsum('bhvk,bhk->bhv', S, r_t)

    xs = tuple(jnp.swapaxes(t, 0, 1) for t in (r, decay, k, v, kk, a))
    S_T, ys = lax.scan(step, wkv0.astype(f32), xs)
    y = jnp.swapaxes(ys, 0, 1)
    mu = jnp.mean(y, -1, keepdims=True)
    yc = y - mu
    y = yc * lax.rsqrt(jnp.mean(yc * yc, -1, keepdims=True) + GN_EPS)
    y = y.reshape(B, T, RWKV_WIDTH) * gn_w + gn_b
    bonus = jnp.sum(r * k * r_k, -1, keepdims=True) * v
    y = (y + bonus.reshape(B, T, RWKV_WIDTH)) * g
    return y, S_T

def token_mixer(x, x_prev_row, k_cache, v_cache, wkv0, w_in, mu_shift, w0, w_lora_up, a0, a_lora_up,
                g_lora_up, k_k, k_a, r_k, gn_w, gn_b, w_out):
    B, T, _ = x.shape
    x_ext = jnp.concatenate([x_prev_row[:, None, :].astype(x.dtype), x], axis=1)
    proj = x_ext @ w_in
    cur = proj[:, 1:]
    q = cur[..., :ATT_WIDTH].reshape(B, T, N_ATT_HEADS, HEAD_DIM)
    k = cur[..., ATT_WIDTH:2 * ATT_WIDTH].reshape(B, T, N_ATT_HEADS, HEAD_DIM)
    v = cur[..., 2 * ATT_WIDTH:3 * ATT_WIDTH].reshape(B, T, N_ATT_HEADS, HEAD_DIM)
    if k_cache is None:
        k_all, v_all, prefix = k, v, 0
    else:
        k_all = jnp.concatenate([k_cache.astype(k.dtype), k], axis=1)
        v_all = jnp.concatenate([v_cache.astype(v.dtype), v], axis=1)
        prefix = k_cache.shape[1]
    att = dilated_window_attention(q, k_all, v_all, prefix)
    rw_cur = cur[..., 3 * ATT_WIDTH:]
    rw_prev = proj[:, :-1, 3 * ATT_WIDTH:]
    rw = rw_cur + (rw_prev - rw_cur) * mu_shift
    y_rw, wkv_T = rwkv7_time_mix(rw, wkv0, w0, w_lora_up, a0, a_lora_up, g_lora_up, k_k, k_a, r_k, gn_w, gn_b)
    mixed = jnp.concatenate([att.reshape(B, T, ATT_WIDTH).astype(jnp.float32), y_rw], axis=-1)
    return mixed.astype(x.dtype) @ w_out, k, v, wkv_T.astype(x.dtype)

def conv_ffn(x, conv_prev, w_ffn_in, conv_w, conv_b, w_ffn_out):
    hu = x @ w_ffn_in
    gate_pre, up = hu[..., :D_FF], hu[..., D_FF:]
    ext = jnp.concatenate([conv_prev.astype(gate_pre.dtype), gate_pre], axis=1)
    c = lax.conv_general_dilated(ext, conv_w[:, None, :].astype(ext.dtype), window_strides=(1,), padding='VALID',
                                 dimension_numbers=('NWC', 'WIO', 'NWC'), feature_group_count=D_FF) + conv_b
    h = jax.nn.silu(c) * up
    return h @ w_ffn_out, ext[:, -(CONV_W - 1):]

def decoder_layer(x, x_prev_row, k_cache, v_cache, wkv0, conv_prev, w_in, mu_shift, w0, w_lora_up, a0,
                  a_lora_up, g_lora_up, k_k, k_a, r_k, gn_w, gn_b, w_out, ln1_g, ln1_b, w_ffn_in, conv_w,
                  conv_b, w_ffn_out, ln2_g, ln2_b):
    h, k_new, v_new, wkv_T = token_mixer(x, x_prev_row, k_cache, v_cache, wkv0, w_in, mu_shift, w0, w_lora_up,
                                         a0, a_lora_up, g_lora_up, k_k, k_a, r_k, gn_w, gn_b, w_out)
    x1 = layer_norm(ALPHA * x + h, ln1_g, ln1_b)
    f, conv_T = conv_ffn(x1, conv_prev, w_ffn_in, conv_w, conv_b, w_ffn_out)
    y = layer_norm(ALPHA * x1 + f, ln2_g, ln2_b)
    return y, k_new, v_new, x[:, -1, :], wkv_T, conv_T

def setup_inputs(seed: int = 0) -> dict:
    key = jax.random.key(seed)
    ks = jax.random.split(key, 32)
    f32 = jnp.float32
    nrm = lambda k, shape, s: s * jax.random.normal(k, shape, f32)
    wbuf = min(MAX_WIN, PAST_LEN)
    col_scale = np.ones((IN_COLS,), np.float32)
    col_scale[2 * ATT_WIDTH:3 * ATT_WIDTH] = BETA
    col_scale[3 * ATT_WIDTH + 2 * RWKV_WIDTH:3 * ATT_WIDTH + 3 * RWKV_WIDTH] = BETA
    L = DEPTH
    return {
        'x_prompt': nrm(ks[0], (BATCH, SEQ, D_MODEL), 1.0),
        'x_sample': nrm(ks[1], (DEC_BATCH, DEC_SEQ, D_MODEL), 1.0),
        'cache_k_win': nrm(ks[2], (L, DEC_BATCH, wbuf, N_ATT_HEADS, HEAD_DIM), 1.0),
        'cache_v_win': nrm(ks[3], (L, DEC_BATCH, wbuf, N_ATT_HEADS, HEAD_DIM), BETA),
        'state_shift': nrm(ks[4], (L, DEC_BATCH, D_MODEL), 1.0),
        'state_wkv': nrm(ks[5], (L, DEC_BATCH, N_RWKV_HEADS, HEAD_DIM, HEAD_DIM), 0.3),
        'state_conv': nrm(ks[6], (L, DEC_BATCH, CONV_W - 1, D_FF), BETA),
        'w_in': nrm(ks[7], (L, D_MODEL, IN_COLS), D_MODEL ** -0.5) * jnp.asarray(col_scale),
        'mu_shift': jax.random.uniform(ks[8], (L, RW_COLS), f32, 0.1, 0.9),
        'w0': jax.random.uniform(ks[9], (L, RWKV_WIDTH), f32, -6.0, -1.0),
        'w_lora_up': nrm(ks[10], (L, DECAY_LORA, RWKV_WIDTH), 0.1 * DECAY_LORA ** -0.5),
        'a0': nrm(ks[11], (L, RWKV_WIDTH), 0.1),
        'a_lora_up': nrm(ks[12], (L, AAA_LORA, RWKV_WIDTH), 0.5 * AAA_LORA ** -0.5),
        'g_lora_up': nrm(ks[13], (L, GATE_LORA, RWKV_WIDTH), GATE_LORA ** -0.5),
        'k_k': 0.85 + nrm(ks[14], (L, RWKV_WIDTH), 0.02),
        'k_a': 1.0 + nrm(ks[15], (L, RWKV_WIDTH), 0.02),
        'r_k': nrm(ks[16], (L, N_RWKV_HEADS, HEAD_DIM), 0.1),
        'gn_w': 1.0 + nrm(ks[17], (L, RWKV_WIDTH), 0.02),
        'gn_b': nrm(ks[18], (L, RWKV_WIDTH), 0.01),
        'w_out': nrm(ks[19], (L, D_MODEL, D_MODEL), BETA * D_MODEL ** -0.5),
        'ln1_g': 1.0 + nrm(ks[20], (L, D_MODEL), 0.02),
        'ln1_b': nrm(ks[21], (L, D_MODEL), 0.01),
        'w_ffn_in': nrm(ks[22], (L, D_MODEL, 2 * D_FF), BETA * D_MODEL ** -0.5),
        'conv_w': nrm(ks[23], (L, CONV_W, D_FF), CONV_W ** -0.5),
        'conv_b': nrm(ks[24], (L, D_FF), 0.01),
        'w_ffn_out': nrm(ks[25], (L, D_FF, D_MODEL), BETA * D_FF ** -0.5),
        'ln2_g': 1.0 + nrm(ks[26], (L, D_MODEL), 0.02),
        'ln2_b': nrm(ks[27], (L, D_MODEL), 0.01),
    }

def reference(x_prompt, x_sample, cache_k_win, cache_v_win, state_shift, state_wkv, state_conv, w_in, mu_shift,
              w0, w_lora_up, a0, a_lora_up, g_lora_up, k_k, k_a, r_k, gn_w, gn_b, w_out, ln1_g, ln1_b, w_ffn_in,
              conv_w, conv_b, w_ffn_out, ln2_g, ln2_b):
    hp, hs = x_prompt, x_sample
    Bp = hp.shape[0]
    kp_l, vp_l, ks_l, vs_l, sp_l, ss_l, wp_l, ws_l, cp_l, cs_l = [], [], [], [], [], [], [], [], [], []
    for l in range(DEPTH):
        lw = (w_in[l], mu_shift[l], w0[l], w_lora_up[l], a0[l], a_lora_up[l], g_lora_up[l], k_k[l], k_a[l],
              r_k[l], gn_w[l], gn_b[l], w_out[l], ln1_g[l], ln1_b[l], w_ffn_in[l], conv_w[l], conv_b[l],
              w_ffn_out[l], ln2_g[l], ln2_b[l])
        zero_row = jnp.zeros((Bp, D_MODEL), hp.dtype)
        zero_wkv = jnp.zeros((Bp, N_RWKV_HEADS, HEAD_DIM, HEAD_DIM), hp.dtype)
        zero_conv = jnp.zeros((Bp, CONV_W - 1, D_FF), hp.dtype)
        x_in_p = hp
        hp, kp, vp, sp, wp, cp = decoder_layer(x_in_p, zero_row, None, None, zero_wkv, zero_conv, *lw)
        hs, kn, vn, sn, wn, cn = decoder_layer(hs, state_shift[l], cache_k_win[l], cache_v_win[l], state_wkv[l],
                                               state_conv[l], *lw)
        n_keep = min(MAX_WIN, kp.shape[1])
        kp_l.append(kp[:, kp.shape[1] - n_keep:])
        vp_l.append(vp[:, vp.shape[1] - n_keep:])
        ks_l.append(kn)
        vs_l.append(vn)
        sp_l.append(sp)
        ss_l.append(sn)
        wp_l.append(wp)
        ws_l.append(wn)
        cp_l.append(cp)
        cs_l.append(cn)
    k_win_prompt = jnp.stack(kp_l)
    v_win_prompt = jnp.stack(vp_l)
    k_new_sample = jnp.stack(ks_l)
    v_new_sample = jnp.stack(vs_l)
    shift_prompt = jnp.stack(sp_l)
    shift_sample = jnp.stack(ss_l)
    wkv_prompt = jnp.stack(wp_l)
    wkv_sample = jnp.stack(ws_l)
    conv_prompt = jnp.stack(cp_l)
    conv_sample = jnp.stack(cs_l)
    return (hp, hs, k_win_prompt, v_win_prompt, k_new_sample, v_new_sample, shift_prompt, shift_sample,
            wkv_prompt, wkv_sample, conv_prompt, conv_sample)


_drawn_inputs = setup_inputs


def setup_inputs(seed=0):
    import zlib

    import numpy as np

    out = dict(_drawn_inputs(seed))
    spreads = {}
    factors = {'w_lora_up': 8.0,
     'k_k': 8.146,
     'gn_w': 26.909,
     'gn_b': 54.001,
     'ln1_g': 8.063,
     'ln1_b': 14.948,
     'conv_b': 31.032,
     'ln2_g': 7.63,
     'ln2_b': 17.294,
     'cache_k_win': 2.867,
     'r_k': 4.464}
    for name, (base, spread) in spreads.items():
        noise = np.random.default_rng([zlib.crc32(name.encode()), seed]).standard_normal(out[name].shape)
        drawn = base * np.exp(spread * noise) if base else spread * noise
        out[name] = __import__('jax').numpy.asarray(drawn.astype(out[name].dtype))
    for name, factor in factors.items():
        out[name] = (out[name] * factor).astype(out[name].dtype)
    return out
```

```python
import math
from contextlib import ExitStack

import numpy as np

import concourse.bass as bass
from concourse import mybir

F32 = mybir.dt.float32
F32R = mybir.dt.float32r
ALU = mybir.AluOpType
ACT = mybir.ActivationFunctionType
AX = mybir.AxisListType.X

P = 128
D = 1024
T = 512
B = 8
HD = 64
H = 8
AW = H * HD
KT = D // P
FF = 2816
FT = FF // P
GL = 160
PAST = 2048
TB = T // P
CC = AW // P
XC = T + 2 * B
XH = XC // 2
TC = T + B
TH = TC // 2
ALPHA = 2.0 ** 0.25
LN_EPS = 1e-5
GN_EPS = 64e-5
DEC = math.exp(-0.5)
NEG = -1e30
N_ATT = 3 * CC
IN_ORDER = list(range(N_ATT)) + [24, 25, 26] + list(range(N_ATT, N_ATT + 3 * CC))
N_IN = len(IN_ORDER)
J_WA, J_G, J_BO, J_R, J_K, J_V = 0, 1, 0, 4, 4 + CC, 4 + 2 * CC
N_RW = N_IN - N_ATT
DOWN = [(0, 8), (8, 15), (15, 22)]
S_OUT = N_IN
S_FF = S_OUT + KT
S_DOWN = S_FF + 2 * FT
N_SLOTS = S_DOWN + 3 * KT
NPAR = N_RW + 7 * CC + 4 * KT + 4 * FT + 2
NSB = 3
NKV = 3
UNITS = TB * H
NLEV = 7

C_MU = 0
C_W0 = C_MU + N_RW
C_A0 = C_W0 + CC
C_KK = C_A0 + CC
C_KA = C_KK + CC
C_RK = C_KA + CC
C_GW = C_RK + CC
C_GB = C_GW + CC
C_L1G = C_GB + CC
C_L1B = C_L1G + KT
C_L2G = C_L1B + KT
C_L2B = C_L2G + KT
C_CW = C_L2B + KT
C_CB = C_CW + 3 * FT
C_EPS = C_CB + FT


def slot_plan():
    plan = [(s, 0, KT, True, True) for s in range(S_DOWN)]
    for m in range(KT):
        for i, (a, b) in enumerate(DOWN):
            plan.append((S_DOWN + m, a, b - a, i == 0, i == len(DOWN) - 1))
    return plan


def shape_constants():
    i = np.arange(P)
    c = {}
    c["ident"] = np.eye(P, dtype=np.float32)
    c["head_sum"] = (i[:, None] // HD == i[None, :] // HD).astype(np.float32)
    c["head_mean"] = c["head_sum"] / HD
    c["all_mean"] = np.full((P, P), 1.0 / D, np.float32)
    lev = np.zeros((P, NLEV, P), np.float32)
    for l in range(NLEV):
        t, s = i[:, None] >> l, i[None, :] >> l
        lev[:, l] = (t % 2 == 1) & (s == t - 1)
    lev[:, 0] = lev[:, 0].T.copy()
    c["level"] = lev
    before, upto = i[:, None] < i[None, :], i[:, None] <= i[None, :]
    c["causal"] = np.concatenate([before, upto, before, upto], 1).astype(np.float32)
    dist = (T - P) + i[:, None] - np.arange(T)[None, :]
    n = (dist >= 0) * ((dist <= 128) * 1 + (dist % 4 == 0) * 1 + (dist % 16 == 0) * 1)
    c["dist"] = dist.astype(np.float32)
    c["lcount"] = np.where(n > 0, np.log(np.maximum(n, 1)), NEG).astype(np.float32)
    far = np.full((NSB, P), -1)
    far[0] = P - i
    far[1, :96] = 512 - 4 * i[:96]
    far[1, 96] = 0
    far[2, :96] = 2048 - 16 * i[:96]
    m = (far <= 128) * 1 + ((far % 4 == 0) & (far <= 512)) * 1 + (far % 16 == 0) * 1
    slope = 2.0 ** -np.arange(1, H + 1)
    sb = np.where(far >= 0, np.log(np.maximum(m, 1)) - slope[:, None, None] * far, NEG)
    c["sbias"] = np.tile(sb.reshape(H, NSB * P), (B, 1)).astype(np.float32)
    return c


def layer(nc, a):
    plan = slot_plan()
    slopes = [2.0 ** -(h + 1) for h in range(H)]
    perm = ExitStack()

    def sem(name):
        return perm.enter_context(nc.semaphore(name))

    def sb(stack, name, shape, dt=F32):
        return stack.enter_context(nc.sbuf_tensor(name, shape, dt))

    banks = perm.enter_context(nc.psum_tensor("banks", [P, 8, 512], F32))

    w_raw = sb(perm, "w_raw", [P, 2, KT * P])
    w_hi = sb(perm, "w_hi", [P, 2, KT * P], F32R)
    w_lo = sb(perm, "w_lo", [P, 2, KT * P], F32R)
    ident = sb(perm, "ident", [P, P])
    all_mean = sb(perm, "all_mean", [P, P])
    par = sb(perm, "par", [P, NPAR])
    mixa_hi = sb(perm, "mixa_hi", [P, CC, TC], F32R)
    mixa_lo = sb(perm, "mixa_lo", [P, CC, TC], F32R)

    def col(k):
        return par[:, k:k + 1]

    mixer = ExitStack()
    head_sum = sb(mixer, "head_sum", [P, P])
    head_mean = sb(mixer, "head_mean", [P, P])
    level = sb(mixer, "level", [P, NLEV, P])
    causal = sb(mixer, "causal", [P, 4 * P])
    rw = sb(mixer, "rw", [P, N_RW + 1, XC])
    low_up = sb(mixer, "low_up", [P, AW])
    gate_up = sb(mixer, "gate_up", [P, 2, AW])

    pa = ExitStack()
    x_hi = sb(pa, "x_hi", [P, KT, XC], F32R)
    x_lo = sb(pa, "x_lo", [P, KT, XC], F32R)
    att = sb(pa, "att", [P, N_ATT, XC])
    pre = sb(pa, "pre", [P, 2, XC + 4])
    dif = sb(pa, "dif", [P, XC])
    dist = sb(pa, "dist", [P, T])
    lcount = sb(pa, "lcount", [P, T])
    alibi = sb(pa, "alibi", [P, T])
    sw = sb(pa, "sw", [P, 2, T])
    pt = sb(pa, "pt", [P, 2, T])
    vtok = sb(pa, "vtok", [P, TB, AW])
    onrm = sb(pa, "onrm", [P, AW])
    nmax = sb(pa, "nmax", [P, UNITS])
    rsum = sb(pa, "rsum", [P, UNITS])
    rinv = sb(pa, "rinv", [P, UNITS])
    kv = sb(pa, "kv", [P, NKV, NSB * AW])
    srow = sb(pa, "srow", [B, 3 * AW])
    sscore = sb(pa, "sscore", [P, NSB, B * H])
    sprob = sb(pa, "sprob", [P, NSB, B * H])
    ssoft = sb(pa, "ssoft", [B * H, NSB * P])
    sbias = sb(pa, "sbias", [B * H, NSB * P])
    sstat = sb(pa, "sstat", [B * H, 4])
    pa.close()

    pb = ExitStack()
    gate = sb(pb, "gate", [P, CC, XC])
    cum = sb(pb, "cum", [P, CC, TB, P + 1])
    kkn = sb(pb, "kkn", [P, CC, XC])
    aa = sb(pb, "aa", [P, CC, XC])
    yy = sb(pb, "yy", [P, CC, XC])
    refs = sb(pb, "refs", [P, 3, CC * TB])
    swk = sb(pb, "swk", [P, 32, HD])
    swt = sb(pb, "swt", [P, 32, HD])
    svec = sb(pb, "svec", [P, 6, HD])
    sval = sb(pb, "sval", [P, 32])
    ssa = sb(pb, "ssa", [P, 2, 32])
    pb1 = ExitStack()
    tmp = sb(pb1, "tmp", [P, 3, XC])
    onemka = sb(pb1, "onemka", [P, CC])
    gath = sb(pb1, "gath", [P, CC, 6, B])
    sixr = sb(pb1, "sixr", [6 * B, AW])
    ones = sb(pb1, "ones", [P, P])
    pb1.close()
    pb2 = ExitStack()
    qq = sb(pb2, "qq", [P, CC, 2, P])
    bk = sb(pb2, "bk", [P, CC, 2, P])
    edec = sb(pb2, "edec", [P, 2, CC, P + 1])
    ms = sb(pb2, "ms", [P, H, 4 * P])
    xx = sb(pb2, "xx", [P, H, 2, P])
    pm = sb(pb2, "pm", [P, H, P])
    btok = sb(pb2, "btok", [P, 2, AW])
    vt = sb(pb2, "vt", [P, TB, AW])
    nr = sb(pb2, "nr", [P, 2, AW // 2])
    uu = sb(pb2, "uu", [P, AW])
    st = sb(pb2, "st", [P, 2, CC * HD])
    escale = sb(pb2, "escale", [P, CC])
    pb2.close()
    pb3 = ExitStack()
    mixb_hi = sb(pb3, "mixb_hi", [P, CC, TC], F32R)
    mixb_lo = sb(pb3, "mixb_lo", [P, CC, TC], F32R)
    tmp3 = sb(pb3, "tmp3", [P, 3, XC])
    yrow = sb(pb3, "yrow", [B, AW])
    mixed_tok = sb(pb3, "mixed_tok", [P, CC, TC])
    pb3.close()
    pb.close()
    mixer.close()

    pc = ExitStack()
    z = sb(pc, "z", [P, KT, TC])
    x1_hi = sb(pc, "x1_hi", [P, KT, TC], F32R)
    x1_lo = sb(pc, "x1_lo", [P, KT, TC], F32R)
    lnt = sb(pc, "lnt", [P, 4, TC])
    tail = sb(pc, "tail", [P, FT, 34])
    GW = T + 2 + B + 3 * B
    gp = sb(pc, "gp", [P, 2, GW])
    cv = sb(pc, "cv", [P, GW])
    act = sb(pc, "act", [P, TC])
    hh = sb(pc, "hh", [P, TC])
    cstate = sb(pc, "cstate", [P, FT, 2 * B])
    h_hi = sb(pc, "h_hi", [P, FT, TC], F32R)
    h_lo = sb(pc, "h_lo", [P, FT, TC], F32R)
    pc.close()

    w_landed = [sem(f"w_landed{i}") for i in range(2)]
    w_hi_ready = sem("w_hi_ready")
    w_lo_ready = sem("w_lo_ready")
    slot_used = sem("slot_used")
    const_landed = sem("const_landed")
    x_landed = sem("x_landed")
    x_hi_ready = sem("x_hi_ready")
    x_lo_ready = sem("x_lo_ready")
    in_copied = sem("in_copied")
    rw_ready = sem("rw_ready")
    pre_zero = sem("pre_zero")
    v_tok_ps = sem("v_tok_ps")
    v_tok = sem("v_tok")
    a_scores = sem("a_scores")
    a_biased = sem("a_biased")
    a_max = sem("a_max")
    a_exp = sem("a_exp")
    a_probs_t = sem("a_probs_t")
    a_pt = sem("a_pt")
    a_pv = sem("a_pv")
    a_norm = sem("a_norm")
    a_back = sem("a_back")
    a_mix_hi = sem("a_mix_hi")
    a_mix_lo = sem("a_mix_lo")
    kv_zero = sem("kv_zero")
    s_rows_ps = sem("s_rows_ps")
    s_rows = sem("s_rows")
    kv_landed = [sem(f"kv_landed{i}") for i in range(NKV)]
    s_qb = sem("s_qb")
    s_prod = sem("s_prod")
    s_red = sem("s_red")
    s_st = sem("s_st")
    s_max = sem("s_max")
    s_exp = sem("s_exp")
    s_prn = sem("s_prn")
    s_pback = sem("s_pback")
    s_prob = sem("s_prob")
    s_pv = sem("s_pv")
    s_mix_hi = sem("s_mix_hi")
    s_mix_lo = sem("s_mix_lo")
    dve = sem("dve_chain")
    act_c = sem("act_chain")
    outs = sem("outs")
    wkv_landed = sem("wkv_landed")
    lo_act = sem("lo_act")
    lora_ps = sem("lora_ps")
    lora_out = sem("lora_out")
    kk_sq = sem("kk_sq")
    kk_ps = sem("kk_ps")
    kk_cl = sem("kk_cl")
    kk_rt = sem("kk_rt")
    kk_done = sem("kk_done")
    bo_in = sem("bo_in")
    bo_ps = sem("bo_ps")
    bo_done = sem("bo_done")
    ga_done = sem("ga_done")
    ga_exp = sem("ga_exp")
    ga_ps = sem("ga_ps")
    ga_row = sem("ga_row")
    sv_landed = sem("sv_landed")
    sw_done = sem("sw_done")
    y_landed = sem("y_landed")
    y_rows_ps = sem("y_rows_ps")
    y_pad = sem("y_pad")
    scan_done = sem("scan_done")
    edec_done = sem("edec_done")
    qb_done = sem("qb_done")
    vt_ps = sem("vt_ps")
    vt_done = sem("vt_done")
    bt_ps = sem("bt_ps")
    bt_done = sem("bt_done")
    sc_ps = sem("sc_ps")
    sc_done = sem("sc_done")
    xt_done = sem("xt_done")
    x0_ps = sem("x0_ps")
    x0_done = sem("x0_done")
    p_ps = sem("p_ps")
    p_done = sem("p_done")
    d_ps = sem("d_ps")
    d_done = sem("d_done")
    r_ps = sem("r_ps")
    r_done = sem("r_done")
    u_ps = sem("u_ps")
    u_done = sem("u_done")
    y_ps = sem("y_ps")
    y_done = sem("y_done")
    st_ps = sem("st_ps")
    st_done = sem("st_done")
    st_zero = sem("st_zero")
    gn_m = sem("gn_m")
    gn_c = sem("gn_c")
    gn_q = sem("gn_q")
    gn_v = sem("gn_v")
    gn_r = sem("gn_r")
    gn_o = sem("gn_o")
    gn_hi = sem("gn_hi")
    gn_lo = sem("gn_lo")
    z_landed = sem("z_landed")
    z_ready = sem("z_ready")
    ln_m = sem("ln_m")
    ln_mc = sem("ln_mc")
    ln_c = sem("ln_c")
    ln_q = sem("ln_q")
    ln_v = sem("ln_v")
    ln_r = sem("ln_r")
    ln_n = sem("ln_n")
    ln_o = sem("ln_o")
    ln_hi = sem("ln_hi")
    ln_lo = sem("ln_lo")
    gp_ready = sem("gp_ready")
    tail_done = sem("tail_done")
    cv_ready = sem("cv_ready")
    act_ready = sem("act_ready")
    hh_ready = sem("hh_ready")
    h_hi_ready = sem("h_hi_ready")
    h_lo_ready = sem("h_lo_ready")

    TICKS = UNITS + 2

    def done(o):
        return o + 1 if o < S_DOWN else S_DOWN + len(DOWN) * (o - S_DOWN + 1)

    def settled(engine):
        count = {}

        def own(signal):
            count[signal.name] = count.get(signal.name, 0) + 1
            engine.wait_ge(signal, count[signal.name])
        return own

    block = perm.enter_context(nc.Block())

    def bank2(o):
        return banks[:, 2 * (o % 2):2 * (o % 2) + 2, :]

    @block.sync
    def _(sp):
        def weights(s):
            _, _, n, _, _ = plan[s]
            if s >= 2:
                sp.wait_ge(w_hi_ready, s - 1)
                sp.wait_ge(w_lo_ready, s - 1)
            sp.dma_start(w_raw[:, s % 2, 0:n * P], a["w"][s, :, 0:n * P]).then_inc(w_landed[s % 2], 16)

        def cache(i):
            src, off = (a["ck"], AW) if i < B else (a["cv"], 2 * AW)
            b, r = i % B, i % NKV
            if i < NKV:
                if i == 0:
                    sp.wait_ge(kv_zero, 1)
                    sp.wait_ge(s_rows, 3)
            elif i - NKV < B:
                sp.wait_ge(s_red, i - NKV + 1)
            else:
                sp.wait_ge(s_pv, i - NKV - B + 1)
            rows = src[b].rearrange("r h d -> r (h d)")
            sp.dma_start(kv[:, r, 0:AW], rows[PAST - P:PAST, :]).then_inc(kv_landed[r], 16)
            sp.dma_start(kv[0:96, r, AW:2 * AW], rows[PAST - 512:PAST - 128:4, :]).then_inc(kv_landed[r], 16)
            sp.dma_start(kv[0:96, r, 2 * AW:3 * AW], rows[0:PAST - 512:16, :]).then_inc(kv_landed[r], 16)
            sp.dma_start(kv[96:97, r, AW:2 * AW], srow[b:b + 1, off:off + AW]).then_inc(kv_landed[r], 16)

        weights(0)
        for n, t in (("ident", ident), ("head_sum", head_sum), ("head_mean", head_mean),
                     ("all_mean", all_mean), ("level", level), ("causal", causal), ("par", par),
                     ("dist", dist), ("lcount", lcount), ("sbias", sbias),
                     ("low_up", low_up), ("gate_up", gate_up)):
            sp.dma_start(t[:], a[n]).then_inc(const_landed, 16)
        sp.dma_start(a["shift_out"], a["x_last"]).then_inc(outs, 16)
        for s in range(1, N_ATT):
            weights(s)
        n_cache = 0
        for s in range(N_ATT, N_IN):
            weights(s)
        sp.wait_ge(in_copied, N_ATT)
        sp.dma_start(a["att_out"], att[:, CC:3 * CC, :]).then_inc(outs, 16)
        for i in range(2 * B):
            cache(i)
        sp.wait_ge(s_mix_lo, 2)
        sp.wait_ge(a_mix_lo, TB)
        sp.wait_ge(slot_used, N_IN)
        sp.wait_ge(outs, 32)
        for v in range(2):
            sp.dma_start(swk[64 * v:64 * v + 64], a["swkv"][:, 32 * v:32 * v + 32, :]).then_inc(wkv_landed, 16)
        sp.wait_ge(ga_row, 1)
        for v in range(2):
            for q in range(6):
                if q == 3:
                    continue
                sp.dma_start(svec[64 * v:64 * v + 64, q, :],
                             sixr[q * B:q * B + B, :].rearrange("b (h k) -> b h k", k=HD)).then_inc(sv_landed, 16)
            sp.dma_start(sval[64 * v:64 * v + 64, :],
                         sixr[3 * B:4 * B, :].rearrange("b (h k) -> b h k", k=HD)[:, :, 32 * v:32 * v + 32])\
                .then_inc(sv_landed, 16)
        sp.wait_ge(sw_done, 1)
        for v in range(2):
            sp.dma_start(a["swkv_out"][:, 32 * v:32 * v + 32, :], swk[64 * v:64 * v + 64]).then_inc(outs, 16)
        sp.wait_ge(sw_done, 2)
        sp.wait_ge(st_done, TB)
        for v in range(2):
            sp.dma_start(yrow[:, :].rearrange("b (h k) -> b h k", k=HD)[:, :, 32 * v:32 * v + 32],
                         ssa[64 * v:64 * v + 64, 1, :]).then_inc(y_landed, 16)
        sp.dma_start(a["wkv_out"], st[:, 0, :]).then_inc(outs, 16)
        for s in range(N_IN, N_IN + 2):
            weights(s)
        sp.wait_ge(gn_lo, 2)
        sp.wait_ge(outs, 80)
        sp.dma_start(z[:, :, :], a["xc"]).then_inc(z_landed, 16)
        sp.dma_start(cstate[:, :, :], a["cstate"]).then_inc(z_landed, 16)
        for s in range(N_IN + 2, N_SLOTS):
            weights(s)
        sp.wait_ge(tail_done, FT)
        sp.dma_start(a["conv_out"], tail[:, :, :]).then_inc(outs, 16)
        for m in range(KT):
            sp.wait_ge(ln_o, KT + m + 1)
            sp.dma_start(a["y_out"][:, m, :], z[:, m, :]).then_inc(outs, 16)
        sp.wait_ge(outs, 16 * (6 + KT))

    @block.gpsimd
    def _(pool):
        own = settled(pool)
        def w_low(s):
            n = plan[s][2]
            pool.wait_ge(w_hi_ready, s + 1)
            pool.tensor_tensor(w_lo[:, s % 2, 0:n * P], w_raw[:, s % 2, 0:n * P],
                               w_hi[:, s % 2, 0:n * P].bitcast(F32), ALU.subtract).then_inc(w_lo_ready, 1)
            own(w_lo_ready)

        pool.memset(pre[:, :, 0:1], 0.0).then_inc(pre_zero, 1)
        own(pre_zero)
        pool.wait_ge(pre_zero, 1)
        pool.memset(kv[96:P, :, :], 0.0).then_inc(kv_zero, 1)
        own(kv_zero)
        pool.wait_ge(kv_zero, 1)
        for s in range(N_IN):
            w_low(s)
        for s in range(N_IN, S_FF):
            w_low(s)
        for f in range(FT):
            w_low(S_FF + 2 * f)
            w_low(S_FF + 2 * f + 1)
            pool.wait_ge(h_hi_ready, f + 1)
            pool.tensor_tensor(h_lo[:, f, :], hh[:, :], h_hi[:, f, :].bitcast(F32), ALU.subtract)\
                .then_inc(h_lo_ready, 1)
            own(h_lo_ready)
        for s in range(S_DOWN, N_SLOTS):
            w_low(s)

    @block.scalar
    def _(ac):
        own = settled(ac)
        def w_high(s):
            n = plan[s][2]
            ac.wait_ge(w_landed[s % 2], 16 * (s // 2 + 1))
            if s >= 2:
                ac.wait_ge(slot_used, s - 1)
            ac.activation(w_hi[:, s % 2, 0:n * P], w_raw[:, s % 2, 0:n * P], ACT.Copy).then_inc(w_hi_ready, 1)
            own(w_hi_ready)

        ac.dma_start(att[:, 0:KT, :], a["x"]).then_inc(x_landed, 16)
        ac.wait_ge(x_landed, 16)
        ac.activation(x_hi[:, :, :], att[:, 0:KT, :], ACT.Copy).then_inc(x_hi_ready, 1)
        own(x_hi_ready)

        def in_copy(o):
            ac.wait_ge(slot_used, done(o))
            ps = bank2(o)[:, :, 0:XH]
            if o < N_ATT:
                if o == 0:
                    ac.wait_ge(x_lo_ready, 1)
                ac.activation(att[:, o, :].rearrange("p (a b) -> p a b", a=2), ps, ACT.Copy).then_inc(in_copied, 1)
                own(in_copied)
            else:
                j = o - N_ATT
                if j >= 2:
                    ac.wait_ge(rw_ready, j - 1)
                ac.activation(pre[:, j % 2, 1:1 + XC].rearrange("p (a b) -> p a b", a=2), ps, ACT.Copy)\
                    .then_inc(in_copied, 1)
                own(in_copied)

        def v_tok_copy(tb):
            ac.wait_ge(v_tok_ps, tb + 1)
            ac.activation(vtok[:, tb, :], banks[:, 5, :], ACT.Copy).then_inc(v_tok, 1)
            own(v_tok)

        def att_exp(u):
            n = (u // H + 1) * P
            ac.wait_ge(a_max, u + 1)
            ac.activation(sw[:, u % 2, 0:n], sw[:, u % 2, 0:n], ACT.Exp, bias=nmax[:, u:u + 1],
                          accum_out=rsum[:, u:u + 1]).then_inc(a_exp, 1)
            own(a_exp)

        def att_mix(q):
            ac.wait_ge(a_back, q + 1)
            ac.activation(mixa_hi[:, :, q * P:q * P + P], banks[:, 6, :].rearrange("p (c t) -> p c t", c=CC),
                          ACT.Copy).then_inc(a_mix_hi, 1)
            own(a_mix_hi)

        def att_tick(k):
            if k < UNITS:
                att_exp(k)
            if k >= 2 and (k - 2) % H == H - 1:
                att_mix((k - 2) // H)

        def rows_copy(i):
            ac.wait_ge(s_rows_ps, i + 1)
            ac.activation(srow[:, i * AW:(i + 1) * AW], banks[0:B, 7, :], ACT.Copy).then_inc(s_rows, 1)
            own(s_rows)

        w_high(0)
        for s in range(N_IN):
            if s + 1 < N_IN:
                w_high(s + 1)
            in_copy(s)
        for tb in range(TB):
            v_tok_copy(tb)
        for i in range(3):
            rows_copy(i)
        for k in range(TICKS):
            att_tick(k)
        ac.wait_ge(s_max, 1)
        ac.activation(ssoft[:, :], ssoft[:, :], ACT.Exp, bias=sstat[:, 0:1], accum_out=sstat[:, 1:2]).then_inc(s_exp, 1)
        own(s_exp)
        ac.wait_ge(s_pback, 1)
        ac.activation(sprob[:, :, :], banks[:, 7, 0:NSB * B * H].rearrange("p (t n) -> p t n", t=NSB), ACT.Copy)\
            .then_inc(s_prob, 1)
        own(s_prob)
        ac.wait_ge(s_pv, B)
        sd = banks[:, 7, 0:CC * B * 2].rearrange("p (c b e) -> p c b e", c=CC, e=2)
        for e in range(2):
            ac.activation(mixa_hi[64 * e:64 * e + 64, :, T:TC], sd[64 * e:64 * e + 64, :, :, e], ACT.Copy)\
                .then_inc(s_mix_hi, 1)
            own(s_mix_hi)

        ac.wait_ge(rw_ready, N_RW)
        ac.activation(rw[0:64, J_WA, :], rw[0:64, J_WA, :], ACT.Tanh).then_inc(lo_act, 1)
        own(lo_act)
        ac.activation(rw[:, J_G:J_G + 2, :], rw[:, J_G:J_G + 2, :], ACT.Sigmoid).then_inc(lo_act, 1)
        own(lo_act)
        ac.wait_ge(s_mix_lo, 2)
        ac.wait_ge(outs, 32)
        for c in range(CC):
            for i, (dst, bias) in enumerate(((yy, C_W0), (aa, C_A0), (gate, None))):
                g = 3 * c + i
                ac.wait_ge(lora_ps, g + 1)
                ps = bank2(g)[:, :, 0:XH]
                o = dst[:, c, :].rearrange("p (a b) -> p a b", a=2)
                if bias is None:
                    ac.activation(o, ps, ACT.Copy).then_inc(lora_out, 1)
                    own(lora_out)
                else:
                    ac.activation(o, ps, ACT.Sigmoid, bias=col(bias + c)).then_inc(lora_out, 1)
                    own(lora_out)
        for c in range(CC):
            ac.wait_ge(kk_cl, c + 1)
            ac.activation(tmp[:, 1, :], tmp[:, 1, :], ACT.Sqrt).then_inc(kk_rt, 1)
            own(kk_rt)
            ac.wait_ge(bo_ps, c + 1)
            ac.activation(rw[:, J_BO + c, :].rearrange("p (a b) -> p a b", a=2),
                          banks[:, 2 * (c % 2):2 * (c % 2) + 2, 0:XH], ACT.Copy).then_inc(bo_done, 1)
            own(bo_done)
        ac.wait_ge(ga_done, 6)
        ac.activation(gath[:, :, 1, :], gath[:, :, 1, :], ACT.Exp, scale=-DEC).then_inc(ga_exp, 1)
        own(ga_exp)
        ac.wait_ge(ga_ps, 1)
        ac.activation(sixr[:, :], banks[0:6 * B, 6, :], ACT.Copy).then_inc(ga_row, 1)
        own(ga_row)

        for n in range(TB):
            ac.wait_ge(scan_done, 2)
            if n == 0:
                ac.wait_ge(sv_landed, 12 * 16)
            if n >= 1:
                ac.wait_ge(qb_done, 4 * n)
                ac.wait_ge(st_done, n)
            for c in range(CC):
                k = c * TB + n
                ac.activation(edec[:, 0, c, :], cum[:, c, n, :], ACT.Exp, scale=-DEC, bias=refs[:, 0, k:k + 1])\
                    .then_inc(edec_done, 1)
                own(edec_done)
                ac.activation(edec[:, 1, c, :], cum[:, c, n, :], ACT.Exp, scale=DEC, bias=refs[:, 1, k:k + 1])\
                    .then_inc(edec_done, 1)
                own(edec_done)
            if n == 0:
                for tb in range(TB):
                    ac.wait_ge(vt_ps, tb + 1)
                    ac.activation(vt[:, tb, :], banks[:, 6 + tb % 2, :], ACT.Copy).then_inc(vt_done, 1)
                    own(vt_done)
            for i in range(2):
                ac.wait_ge(bt_ps, 2 * n + i + 1)
                ac.activation(btok[:, i, :], banks[:, 6 + i, :], ACT.Copy).then_inc(bt_done, 1)
                own(bt_done)
            for g in range(2):
                ac.wait_ge(x0_ps, 2 * n + g + 1)
                ac.activation(xx[:, 4 * g:4 * g + 4, 0, :], banks[:, 4 + g, :].rearrange("p (h s) -> p h s", h=4),
                              ACT.Copy).then_inc(x0_done, 1)
                own(x0_done)
            ac.wait_ge(r_ps, n + 1)
            ac.activation(nr[:, :, :], banks[:, 4:6, 0:AW // 2], ACT.Copy, scale=-1.0).then_inc(r_done, 1)
            own(r_done)
            ac.wait_ge(u_ps, n + 1)
            ac.activation(uu[:, :], banks[:, 6, :], ACT.Copy).then_inc(u_done, 1)
            own(u_done)
            ac.wait_ge(y_ps, n + 1)
            ac.activation(yy[:, :, n * P:n * P + P], banks[:, 7, :].rearrange("p (c t) -> p c t", c=CC), ACT.Copy)\
                .then_inc(y_done, 1)
            own(y_done)
        ac.wait_ge(y_rows_ps, 1)
        ac.activation(yy[:, :, T + 1:XC:2], banks[:, 6, 0:CC * B].rearrange("p (c b) -> p c b", c=CC), ACT.Copy)\
            .then_inc(y_done, 1)
        own(y_done)
        for c in range(CC):
            ac.wait_ge(gn_c, c + 1)
            ac.activation(tmp3[:, 0, :], yy[:, c, :], ACT.Square).then_inc(gn_q, 1)
            own(gn_q)
            ac.wait_ge(gn_v, c + 1)
            ac.activation(tmp3[:, 1, :].rearrange("p (a b) -> p a b", a=2), banks[:, 6:8, 0:XH], ACT.Sqrt,
                          bias=col(C_EPS + 1)).then_inc(gn_r, 1)
            own(gn_r)
        w_high(N_IN)
        w_high(N_IN + 1)
        ac.wait_ge(gn_o, CC)
        ac.activation(mixb_hi[:, :, 0:T], yy[:, :, 0:T], ACT.Copy).then_inc(gn_hi, 1)
        own(gn_hi)
        ac.activation(mixb_hi[:, :, T:TC], yy[:, :, T + 1:XC:2], ACT.Copy).then_inc(gn_hi, 1)
        own(gn_hi)
        for s in range(N_IN + 2, S_FF + 2):
            w_high(s)

        def norm_act(k):
            ac.wait_ge(ln_m, k + 1)
            ac.activation(lnt[:, 0, :].rearrange("p (a b) -> p a b", a=2), banks[:, 4:6, 0:TH], ACT.Copy)\
                .then_inc(ln_mc, 1)
            own(ln_mc)
            for c in range(KT):
                n = k * KT + c
                ac.wait_ge(ln_c, n + 1)
                if n >= 1:
                    ac.wait_ge(ln_v, n)
                ac.activation(lnt[:, 1, :], z[:, c, :], ACT.Square).then_inc(ln_q, 1)
                own(ln_q)
            ac.wait_ge(ln_v, KT * k + KT)
            ac.activation(lnt[:, 2, :].rearrange("p (a b) -> p a b", a=2), banks[:, 6:8, 0:TH], ACT.Sqrt,
                          bias=col(C_EPS)).then_inc(ln_r, 1)
            own(ln_r)
            for c in range(KT):
                n = k * KT + c
                ac.wait_ge(ln_n, n + 1)
                g, b = (C_L1G, C_L1B) if k == 0 else (C_L2G, C_L2B)
                ac.activation(z[:, c, :], z[:, c, :], ACT.Identity, scale=col(g + c), bias=col(b + c))\
                    .then_inc(ln_o, 1)
                own(ln_o)
                if k == 0:
                    ac.wait_ge(ln_o, n + 1)
                    ac.activation(x1_hi[:, c, :], z[:, c, :], ACT.Copy).then_inc(ln_hi, 1)
                    own(ln_hi)

        norm_act(0)
        for f in range(FT):
            o = S_FF + 2 * f
            ac.wait_ge(slot_used, done(o))
            if f >= 2:
                ac.wait_ge(cv_ready, f - 1)
                ac.wait_ge(tail_done, f - 1)
            ac.activation(gp[:, f % 2, 2:2 + TC].rearrange("p (a b) -> p a b", a=2), bank2(o)[:, :, 0:TH], ACT.Copy)\
                .then_inc(gp_ready, 1)
            own(gp_ready)
            w_high(o + 2)
            ac.wait_ge(cv_ready, f + 1)
            if f >= 1:
                ac.wait_ge(hh_ready, f)
            ac.activation(act[:, 0:T], cv[:, 0:T], ACT.Silu).then_inc(act_ready, 1)
            own(act_ready)
            ac.activation(act[:, T:TC], cv[:, T + 2 + B:T + 2 + B + 3 * B:3], ACT.Silu).then_inc(act_ready, 1)
            own(act_ready)
            w_high(o + 3)
            ac.wait_ge(hh_ready, f + 1)
            ac.activation(h_hi[:, f, :], hh[:, :], ACT.Copy).then_inc(h_hi_ready, 1)
            own(h_hi_ready)
        for s in range(S_DOWN + 2, N_SLOTS):
            w_high(s)
        norm_act(1)

    @block.vector
    def _(ve):
        own = settled(ve)
        chain = [0]

        def link(ins):
            chain[0] += 1
            ins.then_inc(dve, 1)
            ve.wait_ge(dve, chain[0])

        def tt(out, a0, a1, op):
            return ve.tensor_tensor(out, a0, a1, op)

        def stt(out, a0, s, a1, op0, op1):
            return ve.scalar_tensor_tensor(out, a0, s, a1, op0, op1)

        ve.wait_ge(x_hi_ready, 1)
        tt(x_lo[:, :, :], att[:, 0:KT, :], x_hi[:, :, :].bitcast(F32), ALU.subtract).then_inc(x_lo_ready, 1)
        own(x_lo_ready)
        ve.wait_ge(const_landed, 16 * 12)
        ve.wait_ge(pre_zero, 1)

        def shift(j):
            ve.wait_ge(in_copied, N_ATT + j + 1)
            cur, prev = pre[:, j % 2, 1:1 + XC], pre[:, j % 2, 0:XC]
            link(tt(dif[:, :], prev, cur, ALU.subtract))
            stt(rw[:, j + (j >= 3), :], dif[:, :], col(C_MU + j), cur, ALU.mult, ALU.add).then_inc(rw_ready, 1)
            own(rw_ready)

        def soft(u):
            q, h = divmod(u, H)
            n = (q + 1) * P
            off = T - n
            link(stt(alibi[:, 0:n], dist[:, off:T], -slopes[h], lcount[:, off:T], ALU.mult, ALU.add))
            ve.wait_ge(a_scores, u + 1)
            if u >= 2:
                ve.wait_ge(a_probs_t, u - 1)
            stt(sw[:, u % 2, 0:n], banks[:, 4, 0:n], HD ** -0.5, alibi[:, 0:n], ALU.mult, ALU.add)\
                .then_inc(a_biased, 1)
            own(a_biased)
            ve.wait_ge(a_biased, u + 1)
            ve.tensor_reduce(nmax[:, u:u + 1], sw[:, u % 2, 0:n], AX, ALU.max, negate=True).then_inc(a_max, 1)
            own(a_max)

        def pt_copy(u):
            n = (u // H + 1) * P
            ve.wait_ge(a_probs_t, u + 1)
            if u >= 2:
                ve.wait_ge(a_pv, u - 1)
            ve.tensor_copy(pt[:, u % 2, 0:n], banks[:, 5, 0:n]).then_inc(a_pt, 1)
            own(a_pt)

        def norm(q):
            ve.wait_ge(a_pv, H * (q + 1))
            link(ve.reciprocal(rinv[:, q * H:(q + 1) * H], rsum[:, q * H:(q + 1) * H]))
            if q >= 1:
                ve.wait_ge(a_back, q)
            tt(onrm[:, :].rearrange("p (h d) -> p h d", d=HD), banks[:, 6, :].rearrange("p (h d) -> p h d", d=HD),
               rinv[:, q * H:(q + 1) * H].unsqueeze(2).broadcast_to([P, H, HD]), ALU.mult).then_inc(a_norm, 1)
            own(a_norm)

        def mix_lo(q):
            ve.wait_ge(a_mix_hi, q + 1)
            tt(mixa_lo[:, :, q * P:q * P + P], banks[:, 6, :].rearrange("p (c t) -> p c t", c=CC),
               mixa_hi[:, :, q * P:q * P + P].bitcast(F32), ALU.subtract).then_inc(a_mix_lo, 1)
            own(a_mix_lo)

        def att_tick(k):
            if k < UNITS:
                soft(k)
            if 1 <= k <= UNITS:
                pt_copy(k - 1)
            if k >= 2 and (k - 2) % H == H - 1:
                norm((k - 2) // H)
                mix_lo((k - 2) // H)

        def s_score(b):
            r = b % NKV
            ve.wait_ge(kv_landed[r], 64 * (b // NKV + 1))
            ve.wait_ge(s_qb, b + 1)
            tt(kv[:, r, :].rearrange("p (t n) -> p t n", t=NSB), kv[:, r, :].rearrange("p (t n) -> p t n", t=NSB),
               banks[:, 7, :].unsqueeze(1).broadcast_to([P, NSB, AW]), ALU.mult).then_inc(s_prod, 1)
            own(s_prod)
            ve.wait_ge(s_prod, b + 1)
            ve.tensor_reduce(sscore[:, :, b * H:(b + 1) * H],
                             kv[:, r, :].rearrange("p (t h d) -> p t h d", t=NSB, d=HD), AX, ALU.add)\
                .then_inc(s_red, 1)
            own(s_red)

        for j in range(N_RW):
            shift(j)
        for k in range(TICKS):
            att_tick(k)
        for b in range(B):
            s_score(b)
        ve.wait_ge(s_st, 1)
        link(stt(ssoft[:, :], banks[0:B * H, 7, 0:NSB * P], HD ** -0.5, sbias[:, :], ALU.mult, ALU.add))
        ve.tensor_reduce(sstat[:, 0:1], ssoft[:, :], AX, ALU.max, negate=True).then_inc(s_max, 1)
        own(s_max)
        ve.wait_ge(s_exp, 1)
        link(ve.reciprocal(sstat[:, 2:3], sstat[:, 1:2]))
        ve.tensor_scalar(ssoft[:, :], ssoft[:, :], sstat[:, 2:3], None, ALU.mult).then_inc(s_prn, 1)
        own(s_prn)
        ve.wait_ge(s_mix_hi, 2)
        sd = banks[:, 7, 0:CC * B * 2].rearrange("p (c b e) -> p c b e", c=CC, e=2)
        for e in range(2):
            tt(mixa_lo[64 * e:64 * e + 64, :, T:TC], sd[64 * e:64 * e + 64, :, :, e],
               mixa_hi[64 * e:64 * e + 64, :, T:TC].bitcast(F32), ALU.subtract).then_inc(s_mix_lo, 1)
            own(s_mix_lo)

        ve.wait_ge(slot_used, N_IN)
        ve.wait_ge(outs, 32)
        link(ve.tensor_scalar(onemka[:, :], par[:, C_KA:C_KA + CC], -1.0, 1.0, ALU.mult, ALU.add))
        link(ve.memset(ones[:, :], 1.0))
        link(ve.memset(cum[:, :, :, 0:1], 0.0))
        for c in range(CC):
            r, k, v = rw[:, J_R + c, :], rw[:, J_K + c, :], rw[:, J_V + c, :]
            ve.tensor_scalar(kkn[:, c, :], k, col(C_KK + c), None, ALU.mult).then_inc(kk_sq, 1)
            own(kk_sq)
            ve.wait_ge(kk_sq, 3 * c + 1)
            if c >= 1:
                ve.wait_ge(kk_ps, c)
            tt(tmp[:, 0, :], kkn[:, c, :], kkn[:, c, :], ALU.mult).then_inc(kk_sq, 1)
            own(kk_sq)
            ve.wait_ge(lora_out, 3 * c + 2)
            if c >= 1:
                ve.wait_ge(bo_ps, c)
            link(ve.tensor_scalar(tmp[:, 2, :], aa[:, c, :], col(C_KA + c), onemka[:, c:c + 1], ALU.mult, ALU.add))
            tt(k, k, tmp[:, 2, :], ALU.mult).then_inc(kk_sq, 1)
            own(kk_sq)
            ve.wait_ge(kk_sq, 3 * c + 3)
            ve.wait_ge(kk_ps, c + 1)
            ve.tensor_scalar(tmp[:, 1, :].rearrange("p (a b) -> p a b", a=2), banks[:, 4:6, 0:XH], 1e-24, None,
                             ALU.max).then_inc(kk_cl, 1)
            own(kk_cl)
            ve.wait_ge(kk_rt, c + 1)
            link(ve.reciprocal(tmp[:, 1, :], tmp[:, 1, :]))
            link(tt(kkn[:, c, :], kkn[:, c, :], tmp[:, 1, :], ALU.mult))
            tt(aa[:, c, :], kkn[:, c, :], aa[:, c, :], ALU.mult).then_inc(kk_done, 1)
            own(kk_done)
            stt(tmp[:, 2, :], r, col(C_RK + c), k, ALU.mult, ALU.mult).then_inc(bo_in, 1)
            own(bo_in)
        ve.wait_ge(kk_done, CC)
        for q, src in enumerate((rw[:, J_R:J_R + CC], yy, rw[:, J_K:J_K + CC], rw[:, J_V:J_V + CC], kkn, aa)):
            if q == 1:
                ve.wait_ge(lora_out, 3 * CC)
            ve.tensor_copy(gath[:, :, q, :], src[:, :, T + 1:XC:2]).then_inc(ga_done, 1)
            own(ga_done)
        for c in range(CC):
            for n in range(TB):
                i = ve.tensor_tensor_scan(cum[:, c, n, 1:P + 1], ones[:, :], yy[:, c, n * P:n * P + P], 0.0,
                                          ALU.mult, ALU.add)
        i.then_inc(scan_done, 1)
        own(scan_done)
        ve.wait_ge(scan_done, 1)
        mid = cum[:, :, :, 64]
        link(ve.tensor_scalar(refs[:, 0, :].rearrange("p (c n) -> p c n", c=CC), mid, DEC, None, ALU.mult))
        ve.tensor_scalar(refs[:, 1, :].rearrange("p (c n) -> p c n", c=CC), mid, -DEC, None, ALU.mult)\
            .then_inc(scan_done, 1)
        own(scan_done)
        ve.wait_ge(wkv_landed, 32)
        ve.wait_ge(sv_landed, 12 * 16)

        def keys(q):
            return svec[:, q, :].unsqueeze(1).broadcast_to([P, 32, HD])

        def vals(x):
            return x.unsqueeze(2).broadcast_to([P, 32, HD])

        link(tt(swt[:, :, :], swk[:, :, :], keys(4), ALU.mult))
        link(ve.tensor_reduce(ssa[:, 0, :], swt[:, :, :], AX, ALU.add))
        link(tt(swk[:, :, :], swk[:, :, :], keys(1), ALU.mult))
        link(tt(swt[:, :, :], vals(ssa[:, 0, :]), keys(5), ALU.mult))
        link(tt(swk[:, :, :], swk[:, :, :], swt[:, :, :], ALU.subtract))
        link(tt(swt[:, :, :], vals(sval[:, :]), keys(2), ALU.mult))
        tt(swk[:, :, :], swk[:, :, :], swt[:, :, :], ALU.add).then_inc(sw_done, 1)
        own(sw_done)
        ve.wait_ge(sw_done, 1)
        link(tt(swt[:, :, :], swk[:, :, :], keys(0), ALU.mult))
        ve.tensor_reduce(ssa[:, 1, :], swt[:, :, :], AX, ALU.add).then_inc(sw_done, 1)
        own(sw_done)

        ve.memset(st[:, 0, :], 0.0).then_inc(st_zero, 1)
        own(st_zero)
        ve.wait_ge(st_zero, 1)
        bf = (0, 1)
        for n in range(TB):
            tok = slice(n * P, n * P + P)
            ve.wait_ge(edec_done, 8 * (n + 1))
            if n >= 1:
                ve.wait_ge(y_ps, n)
            tt(qq[:, :, 0, :], kkn[:, :, tok], edec[:, 0, :, 0:P], ALU.mult).then_inc(qb_done, 1)
            own(qb_done)
            tt(qq[:, :, 1, :], rw[:, J_R:J_R + CC, tok], edec[:, 0, :, 1:P + 1], ALU.mult).then_inc(qb_done, 1)
            own(qb_done)
            tt(bk[:, :, 0, :], aa[:, :, tok], edec[:, 1, :, 1:P + 1], ALU.mult).then_inc(qb_done, 1)
            own(qb_done)
            tt(bk[:, :, 1, :], rw[:, J_K:J_K + CC, tok], edec[:, 1, :, 1:P + 1], ALU.mult).then_inc(qb_done, 1)
            own(qb_done)
            tt(st[:, 1, :].rearrange("p (c v) -> p c v", c=CC), st[:, 0, :].rearrange("p (c v) -> p c v", c=CC),
               edec[:, 1, :, 0:1].broadcast_to([P, CC, HD]), ALU.mult).then_inc(st_zero, 1)
            own(st_zero)
            for h in range(H):
                ve.wait_ge(sc_ps, H * n + h + 1)
                tt(ms[:, h, :], banks[:, h % 4, :], causal[:, :], ALU.mult).then_inc(sc_done, 1)
                own(sc_done)
            for g in range(2):
                hs = slice(4 * g, 4 * g + 4)
                ve.wait_ge(sc_done, H * n + 4 * g + 4)
                link(tt(pm[:, hs, :], ms[:, hs, 0:P], level[:, 0, :].unsqueeze(1).broadcast_to([P, 4, P]), ALU.mult))
                tt(xx[:, hs, 1, :], ident[:, :].unsqueeze(1).broadcast_to([P, 4, P]), pm[:, hs, :], ALU.subtract)\
                    .then_inc(xt_done, 1)
                own(xt_done)
            for l in range(1, NLEV):
                for g in range(2):
                    k = (NLEV - 1) * 2 * n + 2 * (l - 1) + g
                    hs = slice(4 * g, 4 * g + 4)
                    ve.wait_ge(p_ps, k + 1)
                    tt(pm[:, hs, :], banks[:, 4 + g, :].rearrange("p (h s) -> p h s", h=4),
                       level[:, l, :].unsqueeze(1).broadcast_to([P, 4, P]), ALU.mult).then_inc(p_done, 1)
                    own(p_done)
                for g in range(2):
                    k = (NLEV - 1) * 2 * n + 2 * (l - 1) + g
                    hs = slice(4 * g, 4 * g + 4)
                    ve.wait_ge(d_ps, k + 1)
                    tt(xx[:, hs, :, :].rearrange("p h a s -> p (h a s)"), xx[:, hs, :, :].rearrange("p h a s -> p (h a s)"),
                       banks[:, 2 * g:2 * g + 2, :].rearrange("p a b -> p (a b)"), ALU.subtract).then_inc(d_done, 1)
                    own(d_done)
            ve.wait_ge(st_ps, n + 1)
            link(tt(st[:, 1, :], st[:, 1, :], banks[:, 7, 0:CC * HD], ALU.add))
            tt(st[:, 0, :].rearrange("p (c v) -> p c v", c=CC), st[:, 1, :].rearrange("p (c v) -> p c v", c=CC),
               edec[:, 0, :, P:P + 1].broadcast_to([P, CC, HD]), ALU.mult).then_inc(st_done, 1)
            own(st_done)
        ve.wait_ge(y_done, TB)
        ve.memset(yy[:, :, T:XC:2], 0.0).then_inc(y_pad, 1)
        own(y_pad)
        link(tt(rw[:, J_V:J_V + CC, :], rw[:, J_V:J_V + CC, :], rw[:, J_BO:J_BO + CC, :], ALU.mult))
        ve.wait_ge(y_done, TB + 1)
        for c in range(CC):
            ve.wait_ge(gn_m, c + 1)
            y2 = yy[:, c, :].rearrange("p (a b) -> p a b", a=2)
            tt(y2, y2, banks[:, 4:6, 0:XH], ALU.subtract).then_inc(gn_c, 1)
            own(gn_c)
            ve.wait_ge(gn_r, c + 1)
            link(ve.reciprocal(tmp3[:, 2, :], tmp3[:, 1, :]))
            link(tt(yy[:, c, :], yy[:, c, :], tmp3[:, 2, :], ALU.mult))
            link(ve.tensor_scalar(yy[:, c, :], yy[:, c, :], col(C_GW + c), col(C_GB + c), ALU.mult, ALU.add))
            link(tt(yy[:, c, :], yy[:, c, :], rw[:, J_V + c, :], ALU.add))
            tt(yy[:, c, :], yy[:, c, :], gate[:, c, :], ALU.mult).then_inc(gn_o, 1)
            own(gn_o)
        ve.wait_ge(gn_hi, 1)
        tt(mixb_lo[:, :, 0:T], yy[:, :, 0:T], mixb_hi[:, :, 0:T].bitcast(F32), ALU.subtract).then_inc(gn_lo, 1)
        own(gn_lo)
        ve.wait_ge(gn_hi, 2)
        tt(mixb_lo[:, :, T:TC], yy[:, :, T + 1:XC:2], mixb_hi[:, :, T:TC].bitcast(F32), ALU.subtract)\
            .then_inc(gn_lo, 1)
        own(gn_lo)
        ve.wait_ge(z_landed, 32)

        def residual(k, o, c):
            ve.wait_ge(slot_used, done(o))
            z2 = z[:, c, :].rearrange("p (a b) -> p a b", a=2)
            stt(z2, z2, ALPHA, bank2(o)[:, :, 0:TH], ALU.mult, ALU.add).then_inc(z_ready, 1)
            own(z_ready)

        def norm_dve(k):
            ve.wait_ge(ln_mc, k + 1)
            for c in range(KT):
                tt(z[:, c, :], z[:, c, :], lnt[:, 0, :], ALU.subtract).then_inc(ln_c, 1)
                own(ln_c)
            ve.wait_ge(ln_r, k + 1)
            link(ve.reciprocal(lnt[:, 3, :], lnt[:, 2, :]))
            ve.wait_ge(ln_c, KT * k + KT)
            for c in range(KT):
                tt(z[:, c, :], z[:, c, :], lnt[:, 3, :], ALU.mult).then_inc(ln_n, 1)
                own(ln_n)
            if k == 0:
                for c in range(KT):
                    ve.wait_ge(ln_hi, c + 1)
                    tt(x1_lo[:, c, :], z[:, c, :], x1_hi[:, c, :].bitcast(F32), ALU.subtract).then_inc(ln_lo, 1)
                    own(ln_lo)

        for c in range(KT):
            residual(0, S_OUT + c, c)
        norm_dve(0)
        link(ve.memset(gp[:, :, 0:2], 0.0))
        for f in range(FT):
            o = S_FF + 2 * f
            base = T + 2 + B
            g = gp[:, f % 2, :]
            ve.wait_ge(gp_ready, f + 1)
            if f >= 1:
                ve.wait_ge(act_ready, 2 * f)
            tri = gp[:, f % 2, base:GW].rearrange("p (b e) -> p b e", e=3)
            link(ve.tensor_copy(tri[:, :, 0:2], cstate[:, f, :].rearrange("p (b e) -> p b e", e=2)))
            link(ve.tensor_copy(tri[:, :, 2:3], g[:, 2 + T:2 + TC].unsqueeze(2)))
            n = GW - 2
            ve.tensor_copy(tail[:, f, :], g[:, T:GW]).then_inc(tail_done, 1)
            own(tail_done)
            link(ve.tensor_scalar(cv[:, 0:n], g[:, 2:GW], col(C_CW + 2 * FT + f), col(C_CB + f), ALU.mult, ALU.add))
            link(stt(cv[:, 0:n], g[:, 1:GW - 1], col(C_CW + FT + f), cv[:, 0:n], ALU.mult, ALU.add))
            stt(cv[:, 0:n], g[:, 0:n], col(C_CW + f), cv[:, 0:n], ALU.mult, ALU.add).then_inc(cv_ready, 1)
            own(cv_ready)
            ve.wait_ge(act_ready, 2 * f + 2)
            ve.wait_ge(slot_used, done(o + 1))
            if f >= 1:
                ve.wait_ge(h_lo_ready, f)
            tt(hh[:, :].rearrange("p (a b) -> p a b", a=2), act[:, :].rearrange("p (a b) -> p a b", a=2),
               bank2(o + 1)[:, :, 0:TH], ALU.mult).then_inc(hh_ready, 1)
            own(hh_ready)
        for c in range(KT):
            residual(1, S_DOWN + c, c)
        norm_dve(1)

    @block.tensor
    def _(pe):
        def product(s, hi, lo, width, free):
            o, k0, n, first, last = plan[s]
            pe.wait_ge(w_lo_ready, s + 1)
            if first:
                free(o)
            for i in range(n):
                wh, wl = (w[:, s % 2, i * P:(i + 1) * P] for w in (w_hi, w_lo))
                xh, xl = hi(k0 + i), lo(k0 + i)
                for t, (w, x) in enumerate(((wh, xh), (wh, xl), (wl, xh))):
                    for half in range(2):
                        ins = pe.matmul(bank2(o)[:, half, 0:width], w, x[:, half * width:(half + 1) * width],
                                        start=first and i == 0 and t == 0,
                                        stop=last and i == n - 1 and t == 2)
            ins.then_inc(slot_used, 1)

        def mm(out, l, r, start=True, stop=True):
            return pe.matmul(out, l, r, start=start, stop=stop)

        pe.wait_ge(x_hi_ready, 1)
        pe.wait_ge(x_lo_ready, 1)
        pe.wait_ge(const_landed, 16 * 12)
        for s in range(N_IN):
            product(s, lambda k: x_hi[:, k, :], lambda k: x_lo[:, k, :], XH,
                    lambda o: pe.wait_ge(in_copied, o - 1) if o >= 2 else None)
        pe.wait_ge(in_copied, N_ATT)
        for tb in range(TB):
            if tb >= 1:
                pe.wait_ge(v_tok, tb)
            for c in range(CC):
                ins = pe.transpose(banks[:, 5, c * P:(c + 1) * P], att[:, 2 * CC + c, tb * P:tb * P + P], ident[:, :])
            ins.then_inc(v_tok_ps, 1)
        for i in range(3):
            if i >= 1:
                pe.wait_ge(s_rows, i)
            for c in range(CC):
                ins = pe.transpose(banks[0:B, 7, c * P:(c + 1) * P], att[:, i * CC + c, T + 1:XC:2], ident[:, :])
            ins.then_inc(s_rows_ps, 1)

        def scores(u):
            q, h = divmod(u, H)
            lo, n = 64 * (h % 2), (q + 1) * P
            if u >= 1:
                pe.wait_ge(a_biased, u)
            mm(banks[:, 4, 0:n], att[lo:lo + 64, h // 2, q * P:q * P + P], att[lo:lo + 64, CC + h // 2, 0:n])\
                .then_inc(a_scores, 1)

        def probs_t(u):
            pe.wait_ge(a_exp, u + 1)
            if u == 0:
                pe.wait_ge(v_tok, TB)
            else:
                pe.wait_ge(a_pt, u)
            for j in range(u // H + 1):
                ins = pe.transpose(banks[:, 5, j * P:(j + 1) * P], sw[:, u % 2, j * P:(j + 1) * P], ident[:, :])
            ins.then_inc(a_probs_t, 1)

        def values(u):
            q, h = divmod(u, H)
            pe.wait_ge(a_pt, u + 1)
            if h == 0 and q >= 1:
                pe.wait_ge(a_mix_hi, q)
                pe.wait_ge(a_mix_lo, q)
            for j in range(q + 1):
                ins = mm(banks[:, 6, h * HD:(h + 1) * HD], pt[:, u % 2, j * P:(j + 1) * P],
                         vtok[:, j, h * HD:(h + 1) * HD], j == 0, j == q)
            ins.then_inc(a_pv, 1)

        def back(q):
            pe.wait_ge(a_norm, q + 1)
            for c in range(CC):
                ins = pe.transpose(banks[:, 6, c * P:(c + 1) * P], onrm[:, c * P:(c + 1) * P], ident[:, :])
            ins.then_inc(a_back, 1)

        for k in range(TICKS):
            if k < UNITS:
                scores(k)
            if 1 <= k <= UNITS:
                probs_t(k - 1)
            if k >= 2:
                values(k - 2)
                if (k - 2) % H == H - 1:
                    back((k - 2) // H)
        for b in range(B):
            pe.wait_ge(s_rows, 3)
            if b >= 1:
                pe.wait_ge(s_prod, b)
            mm(banks[:, 7, :], ident[0:B, b:b + 1].broadcast_to([B, P]), srow[:, 0:AW]).then_inc(s_qb, 1)
        pe.wait_ge(s_red, B)
        for t in range(NSB):
            ins = pe.transpose(banks[0:B * H, 7, t * P:(t + 1) * P], sscore[:, t, :], ident[:, :])
        ins.then_inc(s_st, 1)
        pe.wait_ge(s_prn, 1)
        for t in range(NSB):
            ins = pe.transpose(banks[:, 7, t * B * H:(t + 1) * B * H], ssoft[:, t * P:(t + 1) * P],
                               ident[0:B * H, 0:B * H])
        ins.then_inc(s_pback, 1)
        pe.wait_ge(s_prob, 1)
        for b in range(B):
            i = B + b
            pe.wait_ge(kv_landed[i % NKV], 64 * (i // NKV + 1))
            for c in range(CC):
                for t in range(NSB):
                    ins = mm(banks[:, 7, (c * B + b) * 2:(c * B + b) * 2 + 2],
                             kv[:, i % NKV, t * AW + c * P:t * AW + (c + 1) * P],
                             sprob[:, t, b * H + 2 * c:b * H + 2 * c + 2], t == 0, t == NSB - 1)
            ins.then_inc(s_pv, 1)
        pe.wait_ge(lo_act, 2)
        for c in range(CC):
            cs = slice(c * P, (c + 1) * P)
            for i in range(3):
                g = 3 * c + i
                if g >= 2:
                    pe.wait_ge(lora_out, g - 1)
                for half in range(2):
                    hs = slice(half * XH, (half + 1) * XH)
                    o = bank2(g)[:, half, 0:XH]
                    if i < 2:
                        ins = mm(o, low_up[64 * i:64 * i + 64, cs], rw[64 * i:64 * i + 64, J_WA, hs])
                    else:
                        mm(o, gate_up[:, 0, cs], rw[:, J_G, hs], True, False)
                        ins = mm(o, gate_up[:, 1, cs], rw[:, J_G + 1, hs], False, True)
                ins.then_inc(lora_ps, 1)
        pe.wait_ge(s_mix_lo, 2)
        pe.wait_ge(lora_out, 3 * CC)
        for c in range(CC):
            pe.wait_ge(kk_sq, 3 * c + 2)
            if c >= 1:
                pe.wait_ge(kk_cl, c)
            for half in range(2):
                ins = mm(banks[:, 4 + half, 0:XH], head_sum[:, :], tmp[:, 0, half * XH:(half + 1) * XH])
            ins.then_inc(kk_ps, 1)
            pe.wait_ge(bo_in, c + 1)
            if c >= 2:
                pe.wait_ge(bo_done, c - 1)
            for half in range(2):
                ins = mm(banks[:, 2 * (c % 2) + half, 0:XH], head_sum[:, :], tmp[:, 2, half * XH:(half + 1) * XH])
            ins.then_inc(bo_ps, 1)
        pe.wait_ge(ga_done, 6)
        pe.wait_ge(ga_exp, 1)
        for c in range(CC):
            ins = pe.transpose(banks[0:6 * B, 6, c * P:(c + 1) * P], gath[:, c, :, :].rearrange("p q b -> p (q b)"),
                               ident[:, :])
        ins.then_inc(ga_ps, 1)
        pe.wait_ge(bo_done, CC)
        pe.wait_ge(ga_row, 1)
        for tb in range(TB):
            if tb >= 2:
                pe.wait_ge(vt_done, tb - 1)
            for c in range(CC):
                ins = pe.transpose(banks[:, 6 + tb % 2, c * P:(c + 1) * P], rw[:, J_V + c, tb * P:tb * P + P],
                                   ident[:, :])
            ins.then_inc(vt_ps, 1)
        pe.wait_ge(vt_done, TB)

        def head(h):
            return 64 * (h % 2), h // 2, slice(h * HD, (h + 1) * HD)

        for n in range(TB):
            pe.wait_ge(qb_done, 4 * n + 4)
            if n >= 1:
                pe.wait_ge(u_done, n)
                pe.wait_ge(st_done, n)
            for i in range(2):
                for c in range(CC):
                    ins = pe.transpose(banks[:, 6 + i, c * P:(c + 1) * P], bk[:, c, i, :], ident[:, :])
                ins.then_inc(bt_ps, 1)
            if n >= 1:
                pe.wait_ge(d_done, 2 * (NLEV - 1) * n)
            for h in range(H):
                lo, c, _ = head(h)
                if h >= 4:
                    pe.wait_ge(sc_done, H * n + h - 3)
                for i in range(2):
                    ins = mm(banks[:, h % 4, 2 * P * i:2 * P * (i + 1)], bk[lo:lo + 64, c, i, :],
                             qq[lo:lo + 64, c, :, :].rearrange("p a t -> p (a t)"))
                ins.then_inc(sc_ps, 1)
            for g in range(2):
                pe.wait_ge(xt_done, 2 * n + g + 1)
                for i in range(4):
                    ins = pe.transpose(banks[:, 4 + g, i * P:(i + 1) * P], xx[:, 4 * g + i, 1, :], ident[:, :])
                ins.then_inc(x0_ps, 1)
            for l in range(1, NLEV):
                for g in range(2):
                    k = (NLEV - 1) * 2 * n + 2 * (l - 1) + g
                    if l == 1:
                        pe.wait_ge(x0_done, 2 * n + g + 1)
                    else:
                        pe.wait_ge(d_done, k - 1)
                    for i in range(4):
                        ins = mm(banks[:, 4 + g, i * P:(i + 1) * P], ms[:, 4 * g + i, 0:P], xx[:, 4 * g + i, 0, :])
                    ins.then_inc(p_ps, 1)
                for g in range(2):
                    k = (NLEV - 1) * 2 * n + 2 * (l - 1) + g
                    pe.wait_ge(p_done, k + 1)
                    for i in range(4):
                        h = 4 * g + i
                        o = banks[:, 2 * g + i // 2, 256 * (i % 2):256 * (i % 2) + 256]
                        mm(o[:, 0:P], xx[:, h, 1, :], pm[:, h, :])
                        ins = mm(o[:, P:2 * P], pm[:, h, :], xx[:, h, 1, :])
                    ins.then_inc(d_ps, 1)
            pe.wait_ge(st_zero, n + 2)
            pe.wait_ge(bt_done, 2 * n + 2)
            pe.wait_ge(d_done, 2 * (NLEV - 1) * (n + 1))
            for h in range(H):
                lo, c, hc = head(h)
                o = banks[:, 4 + h % 2, c * HD:(c + 1) * HD]
                mm(o, qq[lo:lo + 64, c, 0, :], st[lo:lo + 64, 1, c * HD:(c + 1) * HD], True, False)
                ins = mm(o, ms[:, h, 2 * P:3 * P], vt[:, n, hc], False, True)
            ins.then_inc(r_ps, 1)
            pe.wait_ge(r_done, n + 1)
            for h in range(H):
                ins = mm(banks[:, 6, h * HD:(h + 1) * HD], xx[:, h, 1, :], nr[:, h % 2, h // 2 * HD:(h // 2 + 1) * HD])
            ins.then_inc(u_ps, 1)
            pe.wait_ge(u_done, n + 1)
            for h in range(H):
                lo, c, hc = head(h)
                o = banks[lo:lo + 64, 7, c * P:(c + 1) * P]
                mm(o, st[lo:lo + 64, 1, c * HD:(c + 1) * HD], qq[lo:lo + 64, c, 1, :], True, False)
                mm(o, uu[:, hc], ms[:, h, P:2 * P], False, False)
                ins = mm(o, vt[:, n, hc], ms[:, h, 3 * P:4 * P], False, True)
            ins.then_inc(y_ps, 1)
            pe.wait_ge(y_done, n + 1)
            for h in range(H):
                lo, c, hc = head(h)
                o = banks[lo:lo + 64, 7, c * HD:(c + 1) * HD]
                mm(o, btok[:, 0, hc], uu[:, hc], True, False)
                ins = mm(o, btok[:, 1, hc], vt[:, n, hc], False, True)
            ins.then_inc(st_ps, 1)
        pe.wait_ge(y_landed, 32)
        for c in range(CC):
            ins = pe.transpose(banks[:, 6, c * B:(c + 1) * B], yrow[:, c * P:(c + 1) * P], ident[0:B, 0:B])
        ins.then_inc(y_rows_ps, 1)
        pe.wait_ge(y_pad, 1)
        pe.wait_ge(y_done, TB + 1)
        pe.wait_ge(st_done, TB)
        for c in range(CC):
            if c >= 1:
                pe.wait_ge(gn_c, c)
            for half in range(2):
                ins = mm(banks[:, 4 + half, 0:XH], head_mean[:, :], yy[:, c, half * XH:(half + 1) * XH])
            ins.then_inc(gn_m, 1)
            pe.wait_ge(gn_q, c + 1)
            if c >= 1:
                pe.wait_ge(gn_r, c)
            for half in range(2):
                ins = mm(banks[:, 6 + half, 0:XH], head_mean[:, :], tmp3[:, 0, half * XH:(half + 1) * XH])
            ins.then_inc(gn_v, 1)

        def means(c, n):
            pe.wait_ge(z_ready, n)
            for half in range(2):
                ins = mm(banks[:, 4 + half, 0:TH], all_mean[:, :], z[:, c, half * TH:(half + 1) * TH],
                         c == 0, c == KT - 1)
            if c == KT - 1:
                ins.then_inc(ln_m, 1)

        def variances(k):
            for c in range(KT):
                pe.wait_ge(ln_q, KT * k + c + 1)
                for half in range(2):
                    ins = mm(banks[:, 6 + half, 0:TH], all_mean[:, :], lnt[:, 1, half * TH:(half + 1) * TH],
                             c == 0, c == KT - 1)
                ins.then_inc(ln_v, 1)

        pe.wait_ge(gn_lo, 2)
        for c in range(KT):
            product(S_OUT + c, lambda k: mixa_hi[:, k, :] if k < CC else mixb_hi[:, k - CC, :],
                    lambda k: mixa_lo[:, k, :] if k < CC else mixb_lo[:, k - CC, :], TH,
                    lambda o: pe.wait_ge(z_ready, o - S_OUT - 1) if o - S_OUT >= 2 else None)
            if c >= 1:
                means(c - 1, c)
        means(KT - 1, KT)
        variances(0)

        def x1_part(k):
            pe.wait_ge(ln_lo, k + 1)
            return x1_hi[:, k, :]

        def ffn_free(o):
            f, up = divmod(o - S_FF, 2)
            if f == 0:
                pe.wait_ge(z_ready, KT)
            else:
                pe.wait_ge(hh_ready if up else gp_ready, f)

        for s in range(S_FF, S_DOWN):
            product(s, x1_part if s == S_FF else lambda k: x1_hi[:, k, :], lambda k: x1_lo[:, k, :], TH, ffn_free)

        def h_part(k):
            pe.wait_ge(h_lo_ready, k + 1)
            return h_hi[:, k, :]

        def down_free(o):
            m = o - S_DOWN
            if m < 2:
                pe.wait_ge(hh_ready, FT)
                pe.wait_ge(gp_ready, FT)
            else:
                pe.wait_ge(z_ready, KT + m - 1)

        for m in range(KT):
            for i in range(len(DOWN)):
                product(S_DOWN + len(DOWN) * m + i, h_part if m == 0 else lambda k: h_hi[:, k, :],
                        lambda k: h_lo[:, k, :], TH, down_free)
            if m >= 1:
                means(m - 1, KT + m)
        means(KT - 1, 2 * KT)
        variances(1)

    perm.close()


def weight_tiles(w):
    k, m = w.shape
    return w.reshape(k // P, P, m // P, P).transpose(2, 1, 0, 3).reshape(m // P, P, k)


def channel_major(x):
    return x.T.reshape(-1, P, x.shape[0]).transpose(1, 0, 2)


def kernel(**inputs):
    import concourse.bacc as bacc
    from concourse.bass_utils import run_bass_kernel_spmd

    v = {k: np.asarray(x) for k, x in inputs.items()}
    w = {k: x[0] for k, x in v.items() if k not in ("x_prompt", "x_sample")}
    xp, xs = v["x_prompt"][0], v["x_sample"][:, 0]

    pairs = np.stack([w["state_shift"], xs], 1).reshape(2 * B, D)
    w_in = np.concatenate([w["w_in"], np.zeros((D, -w["w_in"].shape[1] % P), np.float32)], 1)
    mu = np.concatenate([w["mu_shift"], np.zeros(-len(w["mu_shift"]) % P, np.float32)])
    w_ff = weight_tiles(w["w_ffn_in"]).reshape(2, FT, P, D).transpose(1, 0, 2, 3).reshape(2 * FT, P, D)
    down = weight_tiles(w["w_ffn_out"])
    slots = np.zeros((N_SLOTS, P, KT * P), np.float32)
    slots[:N_IN] = weight_tiles(w_in)[IN_ORDER]
    slots[S_OUT:S_FF] = weight_tiles(w["w_out"])
    slots[S_FF:S_DOWN] = w_ff
    for i, (k0, k1) in enumerate(DOWN):
        slots[S_DOWN + i::len(DOWN), :, :(k1 - k0) * P] = down[:, :, k0 * P:k1 * P]
    mu_tiles = mu.reshape(-1, P)[[m - N_ATT for m in IN_ORDER[N_ATT:]]]
    rows = [mu_tiles] + [w[n].reshape(-1, P) for n in
                         ("w0", "a0", "k_k", "k_a", "r_k", "gn_w", "gn_b", "ln1_g", "ln1_b", "ln2_g", "ln2_b",
                          "conv_w", "conv_b")]
    rows.append(np.array([[LN_EPS] * P, [GN_EPS] * P], np.float32))
    arrays = shape_constants()
    arrays.update(
        x=channel_major(np.concatenate([xp, pairs])),
        xc=channel_major(np.concatenate([xp, xs])),
        x_last=np.concatenate([xp[-1:], xs]),
        w=slots,
        par=np.concatenate(rows).T,
        low_up=np.concatenate([w["w_lora_up"], w["a_lora_up"]]),
        gate_up=np.concatenate([w["g_lora_up"], np.zeros((2 * P - GL, AW), np.float32)]).reshape(2, P, AW)
        .transpose(1, 0, 2),
        ck=w["cache_k_win"], cv=w["cache_v_win"],
        swkv=w["state_wkv"].reshape(B * H, HD, HD),
        cstate=w["state_conv"].transpose(2, 0, 1).reshape(FT, P, 2 * B).transpose(1, 0, 2),
    )
    arrays = {k: np.ascontiguousarray(x) for k, x in arrays.items()}
    out_shapes = {
        "y_out": (P, KT, TC), "att_out": (P, 2 * CC, XC), "shift_out": (1 + B, D), "wkv_out": (P, CC * HD),
        "swkv_out": (B * H, HD, HD), "conv_out": (P, FT, 34),
    }
    nc = bacc.Bacc("TRN2", target_bir_lowering=False, num_devices=1)
    aps = {k: nc.dram_tensor(f"in_{k}", x.shape, F32, kind="ExternalInput").ap() for k, x in arrays.items()}
    for k, s in out_shapes.items():
        aps[k] = nc.dram_tensor(k, s, F32, kind="ExternalOutput").ap()
    layer(nc, aps)
    r = run_bass_kernel_spmd(nc, [{f"in_{k}": x for k, x in arrays.items()}], core_ids=[0]).results[0]

    def token_major(x):
        return x.transpose(2, 1, 0).reshape(x.shape[2], -1)

    y = token_major(r["y_out"])
    k_all, v_all = token_major(r["att_out"][:, :CC]), token_major(r["att_out"][:, CC:])
    new = slice(T + 1, XC, 2)
    wkv = r["wkv_out"].reshape(2, HD, CC, HD).transpose(2, 0, 3, 1).reshape(H, HD, HD)
    conv = r["conv_out"].transpose(2, 1, 0).reshape(34, FF)
    csample = conv[2 + B:].reshape(B, 3, FF)[:, 1:]
    return (y[None, :T], y[T:, None], k_all[:T].reshape(1, 1, T, H, HD), v_all[:T].reshape(1, 1, T, H, HD),
            k_all[new].reshape(1, B, 1, H, HD), v_all[new].reshape(1, B, 1, H, HD),
            r["shift_out"][None, :1], r["shift_out"][None, 1:], wkv[None, None],
            r["swkv_out"].reshape(1, B, H, HD, HD), conv[None, None, :2], csample[None])
```

```python
import math
from contextlib import ExitStack

import numpy as np

import concourse.bass as bass
from concourse import mybir

F32 = mybir.dt.float32
F32R = mybir.dt.float32r
ALU = mybir.AluOpType
ACT = mybir.ActivationFunctionType
AX = mybir.AxisListType.X

P = 128
D = 1024
T = 512
B = 8
HD = 64
H = 8
AW = H * HD
KT = D // P
FF = 2816
FT = FF // P
GL = 160
PAST = 2048
TB = T // P
CC = AW // P
XC = T + 2 * B
XH = XC // 2
TC = T + B
TH = TC // 2
ALPHA = 2.0 ** 0.25
LN_EPS = 1e-5
GN_EPS = 64e-5
DEC = math.exp(-0.5)
NEG = -1e30
N_ATT = 3 * CC
IN_ORDER = list(range(N_ATT)) + [24, 25, 26] + list(range(N_ATT, N_ATT + 3 * CC))
N_IN = len(IN_ORDER)
J_WA, J_G = 0, 1
J_KK, J_R, J_K, J_V = (3 + i * CC for i in range(4))
N_RW = N_IN - N_ATT
DOWN = [(0, 8), (8, 15), (15, 22)]
S_OUT = N_IN
S_FF = S_OUT + KT
S_DOWN = S_FF + 2 * FT
N_SLOTS = S_DOWN + 3 * KT
NPAR = N_RW + 7 * CC + 4 * KT + 4 * FT + 2 + 4
NSB = 3
NKV = 3
UNITS = TB * H
NLEV = 7

C_MU = 0
C_W0 = C_MU + N_RW
C_A0 = C_W0 + CC
C_KK = C_A0 + CC
C_KA = C_KK + CC
C_RK = C_KA + CC
C_GW = C_RK + CC
C_GB = C_GW + CC
C_L1G = C_GB + CC
C_L1B = C_L1G + KT
C_L2G = C_L1B + KT
C_L2B = C_L2G + KT
C_CW = C_L2B + KT
C_CB = C_CW + 3 * FT
C_EPS = C_CB + FT
C_QUAD = C_EPS + 2


def slot_plan():
    plan = [(s, 0, KT, True, True) for s in range(S_DOWN)]
    for m in range(KT):
        for i, (a, b) in enumerate(DOWN):
            plan.append((S_DOWN + m, a, b - a, i == 0, i == len(DOWN) - 1))
    return plan


def shape_constants():
    i = np.arange(P)
    c = {}
    c["ident"] = np.eye(P, dtype=np.float32)
    c["head_sum"] = (i[:, None] // HD == i[None, :] // HD).astype(np.float32)
    c["head_mean"] = c["head_sum"] / HD
    c["all_mean"] = np.full((P, P), 1.0 / D, np.float32)
    lev = np.zeros((P, NLEV, P), np.float32)
    for l in range(NLEV):
        t, s = i[:, None] >> l, i[None, :] >> l
        lev[:, l] = (t % 2 == 1) & (s == t - 1)
    lev[:, 0] = lev[:, 0].T.copy()
    c["level"] = lev
    before, upto = i[:, None] < i[None, :], i[:, None] <= i[None, :]
    c["causal"] = np.concatenate([before, upto, before, upto], 1).astype(np.float32)
    dist = (T - P) + i[:, None] - np.arange(T)[None, :]
    n = (dist >= 0) * ((dist <= 128) * 1 + (dist % 4 == 0) * 1 + (dist % 16 == 0) * 1)
    c["dist"] = dist.astype(np.float32)
    c["lcount"] = np.where(n > 0, np.log(np.maximum(n, 1)), NEG).astype(np.float32)
    far = np.full((NSB, P), -1)
    far[0] = P - i
    far[1, :96] = 512 - 4 * i[:96]
    far[1, 96] = 0
    far[2, :96] = 2048 - 16 * i[:96]
    m = (far <= 128) * 1 + ((far % 4 == 0) & (far <= 512)) * 1 + (far % 16 == 0) * 1
    slope = 2.0 ** -np.arange(1, H + 1)
    sb = np.where(far >= 0, np.log(np.maximum(m, 1)) - slope[:, None, None] * far, NEG)
    c["sbias"] = np.tile(sb.reshape(H, NSB * P), (B, 1)).astype(np.float32)
    r = i - 40 * (i // 32)
    c["own_head"] = ((r[:, None] == np.arange(AW)[None, :] // HD) & (r[:, None] < H)).astype(np.float32)
    c["quad"] = (i[:, None] // 32 == np.arange(4)).astype(np.float32)
    return c


def layer(nc, a):
    plan = slot_plan()
    slopes = [2.0 ** -(h + 1) for h in range(H)]
    perm = ExitStack()

    def sem(name):
        return perm.enter_context(nc.semaphore(name))

    def sb(stack, name, shape, dt=F32):
        return stack.enter_context(nc.sbuf_tensor(name, shape, dt))

    banks = perm.enter_context(nc.psum_tensor("banks", [P, 8, 512], F32))

    w_raw = sb(perm, "w_raw", [P, 2, KT * P])
    w_hi = sb(perm, "w_hi", [P, 2, KT * P], F32R)
    w_lo = sb(perm, "w_lo", [P, 2, KT * P], F32R)
    ident = sb(perm, "ident", [P, P])
    all_mean = sb(perm, "all_mean", [P, P])
    par = sb(perm, "par", [P, NPAR])
    mixa_hi = sb(perm, "mixa_hi", [P, CC, TC], F32R)
    mixa_lo = sb(perm, "mixa_lo", [P, CC, TC], F32R)

    def col(k):
        return par[:, k:k + 1]

    mixer = ExitStack()
    head_sum = sb(mixer, "head_sum", [P, P])
    head_mean = sb(mixer, "head_mean", [P, P])
    level = sb(mixer, "level", [P, NLEV, P])
    causal = sb(mixer, "causal", [P, 4 * P])
    rw = sb(mixer, "rw", [P, N_RW + CC, XC])
    low_up = sb(mixer, "low_up", [P, AW])
    gate_up = sb(mixer, "gate_up", [P, 2, AW])

    pa = ExitStack()
    x_hi = sb(pa, "x_hi", [P, KT, XC], F32R)
    x_lo = sb(pa, "x_lo", [P, KT, XC], F32R)
    att = sb(pa, "att", [P, N_ATT, XC])
    pre = sb(pa, "pre", [P, 2, XC + 4])
    dist = sb(pa, "dist", [P, T])
    lcount = sb(pa, "lcount", [P, T])
    sw = sb(pa, "sw", [P, 2, T])
    pt = sb(pa, "pt", [P, 2, T])
    vtok = sb(pa, "vtok", [P, TB, AW])
    onrm = sb(pa, "onrm", [P, AW])
    nmax = sb(pa, "nmax", [P, UNITS])
    rsum = sb(pa, "rsum", [P, UNITS])
    rinv = sb(pa, "rinv", [P, UNITS])
    kv = sb(pa, "kv", [P, NKV, NSB * AW])
    srow = sb(pa, "srow", [B, 3 * AW])
    qs = sb(pa, "qs", [P, AW])
    sscore = sb(pa, "sscore", [P, NSB, B * H])
    sprob = sb(pa, "sprob", [P, NSB, B * H])
    ssoft = qs[0:B * H, 0:NSB * P]
    sbias = sb(pa, "sbias", [B * H, NSB * P])
    sstat = sb(pa, "sstat", [B * H, 4])
    pa.close()

    pb = ExitStack()
    cum = sb(pb, "cum", [P, CC, TB, P + 1])
    aa = sb(pb, "aa", [P, CC, XC])
    yy = sb(pb, "yy", [P, CC, XC])
    vt = sb(pb, "vt", [P, TB, AW])
    refs = sb(pb, "refs", [P, 2, CC * TB])
    ends = sb(pb, "ends", [P, 2, CC * TB])
    swt = sb(pb, "swt", [P, 32, HD])
    svec = sb(pb, "svec", [P, 6, HD])
    sval = sb(pb, "sval", [P, 32])
    ssa = sb(pb, "ssa", [P, 2, 32])
    gath = sb(pb, "gath", [P, CC, 6, B])
    sixr = sb(pb, "sixr", [6 * B, AW])
    yrow = sb(pb, "yrow", [B, AW])
    swk = w_raw[:, :, :].rearrange("p a n -> p (a n)").rearrange("p (v k) -> p v k", k=HD)
    pb1 = ExitStack()
    tmp = sb(pb1, "tmp", [P, 3, XC])
    onemka = sb(pb1, "onemka", [P, CC])
    ones = sb(pb1, "ones", [P, P])
    pb1.close()
    pb2 = ExitStack()
    edec = sb(pb2, "edec", [P, 2, CC, P + 1])
    ms = sb(pb2, "ms", [P, 2, H, 4 * P])
    xx = sb(pb2, "xx", [P, H, 2, P])
    xf = sb(pb2, "xf", [P, H, P])
    pm = sb(pb2, "pm", [P, H, P])
    btok = sb(pb2, "btok", [P, 2, AW])
    nr = sb(pb2, "nr", [P, 2, AW // 2])
    uu = sb(pb2, "uu", [P, AW])
    st = sb(pb2, "st", [P, 2, CC * HD])
    pb2.close()
    pb3 = ExitStack()
    mixb_hi = sb(pb3, "mixb_hi", [P, CC, TC], F32R)
    mixb_lo = sb(pb3, "mixb_lo", [P, CC, TC], F32R)
    sq = sb(pb3, "sq", [P, 2, XC])
    sd = sb(pb3, "sd", [P, 2, XC])
    rsd = sb(pb3, "rsd", [P, XC])
    pb3.close()
    pb.close()
    mixer.close()

    pc = ExitStack()
    z = sb(pc, "z", [P, KT, TC])
    x1_hi = sb(pc, "x1_hi", [P, KT, TC], F32R)
    x1_lo = sb(pc, "x1_lo", [P, KT, TC], F32R)
    lsq = sb(pc, "lsq", [P, 2, TC])
    lsd = sb(pc, "lsd", [P, TC])
    lrs = sb(pc, "lrs", [P, TC])
    tail = sb(pc, "tail", [P, FT, 34])
    GW = T + 2 + B + 3 * B
    gp = sb(pc, "gp", [P, 2, GW])
    cv = sb(pc, "cv", [P, GW])
    act = sb(pc, "act", [P, TC])
    hh = sb(pc, "hh", [P, TC])
    cstate = sb(pc, "cstate", [P, FT, 2 * B])
    h_hi = sb(pc, "h_hi", [P, FT, TC], F32R)
    h_lo = sb(pc, "h_lo", [P, FT, TC], F32R)
    pc.close()

    w_landed = [sem(f"w_landed{i}") for i in range(2)]
    w_hi_ready = sem("w_hi_ready")
    w_lo_ready = sem("w_lo_ready")
    slot_used = sem("slot_used")
    const_landed = sem("const_landed")
    x_landed = [sem(f"x_landed{k}") for k in range(KT)]
    x_hi_ready = sem("x_hi_ready")
    x_lo_ready = sem("x_lo_ready")
    in_copied = sem("in_copied")
    rw_ready = sem("rw_ready")
    pre_zero = sem("pre_zero")
    v_tok_ps = sem("v_tok_ps")
    v_tok = sem("v_tok")
    a_scores = sem("a_scores")
    a_biased = sem("a_biased")
    a_max = sem("a_max")
    a_exp = sem("a_exp")
    a_probs_t = sem("a_probs_t")
    a_pt = sem("a_pt")
    a_pv = sem("a_pv")
    a_norm = sem("a_norm")
    a_back = sem("a_back")
    a_mix_hi = sem("a_mix_hi")
    a_mix_lo = sem("a_mix_lo")
    kv_zero = sem("kv_zero")
    s_rows_ps = sem("s_rows_ps")
    s_rows = sem("s_rows")
    kv_landed = [sem(f"kv_landed{i}") for i in range(NKV)]
    s_qb = sem("s_qb")
    s_prod = sem("s_prod")
    s_qs = sem("s_qs")
    s_own = sem("s_own")
    s_own_landed = sem("s_own_landed")
    s_sum = sem("s_sum")
    vb_done = sem("vb_done")
    s_red = sem("s_red")
    s_st = sem("s_st")
    s_max = sem("s_max")
    s_exp = sem("s_exp")
    s_prn = sem("s_prn")
    s_pback = sem("s_pback")
    s_prob = sem("s_prob")
    s_pv = sem("s_pv")
    s_mix_hi = sem("s_mix_hi")
    s_mix_lo = sem("s_mix_lo")
    dve = sem("dve_chain")
    act_c = sem("act_chain")
    outs = sem("outs")
    state_left = sem("state_left")
    wkv_landed = sem("wkv_landed")
    lo_act = sem("lo_act")
    lora_ps = sem("lora_ps")
    lora_out = sem("lora_out")
    kk_in = sem("kk_in")
    kk_sq = sem("kk_sq")
    kk_ps = sem("kk_ps")
    kk_cl = sem("kk_cl")
    kk_rt = sem("kk_rt")
    kk_done = sem("kk_done")
    ends_in = sem("ends_in")
    ends_done = sem("ends_done")
    sw_a = sem("sw_a")
    sw_sa = sem("sw_sa")
    sw_y = sem("sw_y")
    gate_ps = sem("gate_ps")
    bo_in = sem("bo_in")
    bo_ps = sem("bo_ps")
    bo_done = sem("bo_done")
    ga_done = sem("ga_done")
    ga_exp = sem("ga_exp")
    ga_ps = sem("ga_ps")
    ga_row = sem("ga_row")
    sv_landed = sem("sv_landed")
    sw_done = sem("sw_done")
    y_landed = sem("y_landed")
    y_rows_ps = sem("y_rows_ps")
    y_pad = sem("y_pad")
    y_dec = sem("y_dec")
    scan_done = sem("scan_done")
    edec_done = sem("edec_done")
    qb_done = sem("qb_done")
    vt_ps = sem("vt_ps")
    vt_done = sem("vt_done")
    bt_ps = sem("bt_ps")
    bt_done = sem("bt_done")
    sc_ps = sem("sc_ps")
    sc_done = sem("sc_done")
    xt_done = sem("xt_done")
    x0_ps = sem("x0_ps")
    x0_done = sem("x0_done")
    p_ps = sem("p_ps")
    p_done = sem("p_done")
    d_ps = sem("d_ps")
    d_done = sem("d_done")
    r_ps = sem("r_ps")
    r_done = sem("r_done")
    u_ps = sem("u_ps")
    u_done = sem("u_done")
    y_ps = sem("y_ps")
    y_done = sem("y_done")
    st_ps = sem("st_ps")
    st_done = sem("st_done")
    st_zero = sem("st_zero")
    gn_m = sem("gn_m")
    gn_c = sem("gn_c")
    gn_q = sem("gn_q")
    gn_v = sem("gn_v")
    gn_r = sem("gn_r")
    gn_o = sem("gn_o")
    gn_hi = sem("gn_hi")
    gn_lo = sem("gn_lo")
    z_landed = sem("z_landed")
    z_ready = sem("z_ready")
    ln_m = sem("ln_m")
    ln_c = sem("ln_c")
    ln_q = sem("ln_q")
    ln_v = sem("ln_v")
    ln_r = sem("ln_r")
    ln_n = sem("ln_n")
    ln_o = sem("ln_o")
    ln_hi = sem("ln_hi")
    ln_lo_even = sem("ln_lo_even")
    ln_lo_odd = sem("ln_lo_odd")
    gp_ready = sem("gp_ready")
    tail_done = sem("tail_done")
    cv_ready = sem("cv_ready")
    act_ready = sem("act_ready")
    hh_ready = sem("hh_ready")
    h_hi_ready = sem("h_hi_ready")
    h_lo_ready = sem("h_lo_ready")

    TICKS = UNITS + 2
    FIRST_TICK = N_ATT + 2
    PER_SLOT = 3

    def ticks(s):
        k = (s - FIRST_TICK) * PER_SLOT
        return range(max(k, 0), min(max(k + PER_SLOT, 0), TICKS))

    def decode_row(s):
        b = s - FIRST_TICK - 1
        return b if 0 <= b < B else None

    def done(o):
        return o + 1 if o < S_DOWN else S_DOWN + len(DOWN) * (o - S_DOWN + 1)

    def settled(engine):
        count = {}

        def own(signal):
            count[signal.name] = count.get(signal.name, 0) + 1
            engine.wait_ge(signal, count[signal.name])
        return own

    block = perm.enter_context(nc.Block())

    def bank2(o):
        return banks[:, 2 * (o % 2):2 * (o % 2) + 2, :]

    @block.sync
    def _(sp):
        def weights(s):
            _, _, n, _, _ = plan[s]
            if s >= 2:
                sp.wait_ge(w_hi_ready, s - 1)
                sp.wait_ge(w_lo_ready, s - 1)
            sp.dma_start(w_raw[:, s % 2, 0:n * P], a["w"][s, :, 0:n * P]).then_inc(w_landed[s % 2], 16)

        def cache(i):
            src, off = (a["ck"], AW) if i < B else (a["cv"], 2 * AW)
            b, r = i % B, i % NKV
            if i < NKV:
                if i == 0:
                    sp.wait_ge(kv_zero, 1)
                    sp.wait_ge(s_rows, 3)
            elif i - NKV < B:
                sp.wait_ge(s_red, i - NKV + 1)
            else:
                sp.wait_ge(s_pv, i - NKV - B + 1)
            rows = src[b].rearrange("r h d -> r (h d)")
            sp.dma_start(kv[:, r, 0:AW], rows[PAST - P:PAST, :]).then_inc(kv_landed[r], 16)
            sp.dma_start(kv[0:96, r, AW:2 * AW], rows[PAST - 512:PAST - 128:4, :]).then_inc(kv_landed[r], 16)
            sp.dma_start(kv[0:96, r, 2 * AW:3 * AW], rows[0:PAST - 512:16, :]).then_inc(kv_landed[r], 16)
            sp.dma_start(kv[96:97, r, AW:2 * AW], srow[b:b + 1, off:off + AW]).then_inc(kv_landed[r], 16)

        weights(0)
        weights(1)
        for n, t in (("ident", ident), ("par", par), ("head_sum", head_sum), ("head_mean", head_mean),
                     ("all_mean", all_mean), ("level", level), ("causal", causal),
                     ("dist", dist), ("lcount", lcount), ("sbias", sbias),
                     ("low_up", low_up), ("gate_up", gate_up)):
            sp.dma_start(t[:], a[n]).then_inc(const_landed, 16)
        sp.dma_start(a["shift_out"], a["x_last"]).then_inc(outs, 16)
        for s in range(2, N_IN):
            weights(s)
            if s == FIRST_TICK + 2:
                for i in range(NKV):
                    cache(i)
                sp.dma_start(a["att_out"], att[:, CC:3 * CC, :]).then_inc(outs, 16)
            if s >= FIRST_TICK + 5:
                cache(s - FIRST_TICK - 5 + NKV)
        sp.wait_ge(a_pv, UNITS)
        sp.dma_start(pt[:, 0, :], a["own_head"]).then_inc(s_own_landed, 16)
        for i in range(N_IN - FIRST_TICK - 5 + NKV, 2 * B):
            cache(i)
        sp.wait_ge(w_hi_ready, N_IN)
        sp.wait_ge(w_lo_ready, N_IN)
        for v in range(2):
            sp.dma_start(swk[64 * v:64 * v + 64], a["swkv"][:, 32 * v:32 * v + 32, :]).then_inc(wkv_landed, 16)
        sp.wait_ge(ga_row, 1)
        for v in range(2):
            for q in range(6):
                if q == 3:
                    continue
                sp.dma_start(svec[64 * v:64 * v + 64, q, :],
                             sixr[q * B:q * B + B, :].rearrange("b (h k) -> b h k", k=HD)).then_inc(sv_landed, 16)
            sp.dma_start(sval[64 * v:64 * v + 64, :],
                         sixr[3 * B:4 * B, :].rearrange("b (h k) -> b h k", k=HD)[:, :, 32 * v:32 * v + 32])\
                .then_inc(sv_landed, 16)
        sp.wait_ge(sw_a, 6)
        for v in range(2):
            sp.dma_start(a["swkv_out"][:, 32 * v:32 * v + 32, :], swk[64 * v:64 * v + 64]).then_inc(state_left, 16)
        sp.wait_ge(sw_y, 1)
        for v in range(2):
            sp.dma_start(yrow[:, :].rearrange("b (h k) -> b h k", k=HD)[:, :, 32 * v:32 * v + 32],
                         ssa[64 * v:64 * v + 64, 1, :]).then_inc(y_landed, 16)
        sp.wait_ge(st_done, TB)
        sp.dma_start(a["wkv_out"], st[:, 0, :]).then_inc(outs, 16)
        sp.wait_ge(state_left, 32)
        for s in range(N_IN, N_IN + 2):
            weights(s)
        sp.wait_ge(gn_lo, CC)
        sp.wait_ge(outs, 48)
        sp.dma_start(z[:, :, :], a["xc"]).then_inc(z_landed, 16)
        sp.dma_start(cstate[:, :, :], a["cstate"]).then_inc(z_landed, 16)
        for s in range(N_IN + 2, N_SLOTS):
            weights(s)
        sp.wait_ge(tail_done, FT)
        sp.dma_start(a["conv_out"], tail[:, :, :]).then_inc(outs, 16)
        for m in range(KT):
            sp.wait_ge(ln_o, KT + m + 1)
            sp.dma_start(a["y_out"][:, m, :], z[:, m, :]).then_inc(outs, 16)
        sp.wait_ge(outs, 16 * (4 + KT))

    @block.gpsimd
    def _(pool):
        own = settled(pool)
        def w_low(s):
            n = plan[s][2]
            pool.wait_ge(w_hi_ready, s + 1)
            pool.tensor_tensor(w_lo[:, s % 2, 0:n * P], w_raw[:, s % 2, 0:n * P],
                               w_hi[:, s % 2, 0:n * P].bitcast(F32), ALU.subtract).then_inc(w_lo_ready, 1)
            own(w_lo_ready)

        pool.memset(pre[:, :, 0:1], 0.0).then_inc(pre_zero, 1)
        own(pre_zero)
        pool.wait_ge(pre_zero, 1)
        pool.memset(kv[96:P, :, :], 0.0).then_inc(kv_zero, 1)
        own(kv_zero)
        pool.wait_ge(kv_zero, 1)
        def products(b):
            r = b % NKV
            pool.wait_ge(kv_landed[r], 64 * (b // NKV + 1))
            pool.wait_ge(s_qs, b + 1)
            rows = kv[:, r, :].rearrange("p (t n) -> p t n", t=NSB)
            pool.tensor_tensor(rows, rows, qs[:, :].unsqueeze(1).broadcast_to([P, NSB, AW]), ALU.mult)\
                .then_inc(s_prod, 1)
            own(s_prod)

        for s in range(N_IN):
            w_low(s)
            if s > 0 and decode_row(s - 1) is not None:
                products(decode_row(s - 1))

        def keys(q):
            return svec[:, q, :].unsqueeze(1).broadcast_to([P, 32, HD])

        def vals(x):
            return x.unsqueeze(2).broadcast_to([P, 32, HD])

        def step(out, a0, a1, op):
            pool.tensor_tensor(out, a0, a1, op).then_inc(sw_a, 1)
            own(sw_a)

        pool.wait_ge(wkv_landed, 32)
        pool.wait_ge(sv_landed, 12 * 16)
        step(swt[:, :, :], swk, keys(4), ALU.mult)
        step(swk, swk, keys(1), ALU.mult)
        pool.wait_ge(sw_sa, 1)
        step(swt[:, :, :], vals(ssa[:, 0, :]), keys(5), ALU.mult)
        step(swk, swk, swt[:, :, :], ALU.subtract)
        step(swt[:, :, :], vals(sval[:, :]), keys(2), ALU.mult)
        step(swk, swk, swt[:, :, :], ALU.add)
        step(swt[:, :, :], swk, keys(0), ALU.mult)
        for s in range(N_IN, S_FF):
            w_low(s)
        w_low(S_FF)
        w_low(S_FF + 1)
        for c in range(0, KT, 2):
            pool.wait_ge(ln_hi, c + 1)
            pool.tensor_tensor(x1_lo[:, c, :], z[:, c, :], x1_hi[:, c, :].bitcast(F32), ALU.subtract)\
                .then_inc(ln_lo_even, 1)
            own(ln_lo_even)
        for s in range(S_FF + 2, N_SLOTS):
            w_low(s)

    @block.scalar
    def _(ac):
        own = settled(ac)
        def w_high(s):
            n = plan[s][2]
            ac.wait_ge(w_landed[s % 2], 16 * (s // 2 + 1))
            if s >= 2:
                ac.wait_ge(slot_used, s - 1)
            ac.activation(w_hi[:, s % 2, 0:n * P], w_raw[:, s % 2, 0:n * P], ACT.Copy).then_inc(w_hi_ready, 1)
            own(w_hi_ready)

        for k in range(KT):
            ac.dma_start(att[:, k, :], a["x"][:, k, :]).then_inc(x_landed[k], 16)
        w_high(0)
        for k in range(KT):
            ac.wait_ge(x_landed[k], 16)
            ac.activation(x_hi[:, k, :], att[:, k, :], ACT.Copy).then_inc(x_hi_ready, 1)
            own(x_hi_ready)

        def in_copy(o):
            ac.wait_ge(slot_used, done(o))
            ps = bank2(o)[:, :, 0:XH]
            if o < N_ATT:
                if o == 0:
                    ac.wait_ge(x_lo_ready, KT)
                ac.activation(att[:, o, :].rearrange("p (a b) -> p a b", a=2), ps, ACT.Copy).then_inc(in_copied, 1)
                own(in_copied)
            else:
                j = o - N_ATT
                if j >= 2:
                    ac.wait_ge(rw_ready, j - 1)
                ac.activation(pre[:, j % 2, 1:1 + XC].rearrange("p (a b) -> p a b", a=2), ps, ACT.Copy)\
                    .then_inc(in_copied, 1)
                own(in_copied)

        def v_tok_copy(tb):
            ac.wait_ge(v_tok_ps, tb + 1)
            ac.activation(vtok[:, tb, :], banks[:, 5, :], ACT.Copy).then_inc(v_tok, 1)
            own(v_tok)

        def att_exp(u):
            n = (u // H + 1) * P
            ac.wait_ge(a_max, u + 1)
            ac.activation(sw[:, u % 2, 0:n], sw[:, u % 2, 0:n], ACT.Exp, bias=nmax[:, u:u + 1],
                          accum_out=rsum[:, u:u + 1]).then_inc(a_exp, 1)
            own(a_exp)

        def pt_copy(u):
            n = (u // H + 1) * P
            ac.wait_ge(a_probs_t, u + 1)
            if u >= 2:
                ac.wait_ge(a_pv, u - 1)
            ac.activation(pt[:, u % 2, 0:n], banks[:, 5, 0:n], ACT.Copy).then_inc(a_pt, 1)
            own(a_pt)

        def spread_copy(b):
            ac.wait_ge(s_qb, b + 1)
            if b >= 1:
                ac.wait_ge(s_prod, b)
            ac.activation(qs[:, :], banks[:, 7, :], ACT.Copy).then_inc(s_qs, 1)
            own(s_qs)

        def att_mix(q):
            ac.wait_ge(a_back, q + 1)
            ac.activation(mixa_hi[:, :, q * P:q * P + P], banks[:, 6, :].rearrange("p (c t) -> p c t", c=CC),
                          ACT.Copy).then_inc(a_mix_hi, 1)
            own(a_mix_hi)

        def att_tick(k):
            if 1 <= k <= UNITS:
                pt_copy(k - 1)
            if k < UNITS:
                att_exp(k)
            if k >= 2 and (k - 2) % H == H - 1:
                att_mix((k - 2) // H)

        def rows_copy(i):
            ac.wait_ge(s_rows_ps, i + 1)
            ac.activation(srow[:, i * AW:(i + 1) * AW], banks[0:B, 7, :], ACT.Copy).then_inc(s_rows, 1)
            own(s_rows)

        for s in range(N_IN + 1):
            if s >= 1:
                in_copy(s - 1)
            if s + 1 < N_IN:
                w_high(s + 1)
            if s == FIRST_TICK - 1:
                for tb in range(TB):
                    v_tok_copy(tb)
                for i in range(3):
                    rows_copy(i)
            for i, k in enumerate(ticks(s)):
                att_tick(k)
                if i == 0 and decode_row(s) is not None:
                    spread_copy(decode_row(s))
        ac.wait_ge(s_max, 1)
        ac.activation(ssoft[:, :], ssoft[:, :], ACT.Exp, bias=sstat[:, 0:1], accum_out=sstat[:, 1:2]).then_inc(s_exp, 1)
        own(s_exp)
        ac.wait_ge(rw_ready, N_RW)
        ac.activation(rw[0:64, J_WA, :], rw[0:64, J_WA, :], ACT.Tanh).then_inc(lo_act, 1)
        own(lo_act)
        ac.activation(rw[:, J_G:J_G + 2, :], rw[:, J_G:J_G + 2, :], ACT.Sigmoid).then_inc(lo_act, 1)
        own(lo_act)
        ac.wait_ge(slot_used, N_IN)
        ac.wait_ge(outs, 32)
        for c in range(CC):
            for i, (dst, bias) in enumerate(((yy, C_W0), (aa, C_A0))):
                g = 2 * c + i
                ac.wait_ge(lora_ps, g + 1)
                ac.activation(dst[:, c, :].rearrange("p (a b) -> p a b", a=2), bank2(g)[:, :, 0:XH], ACT.Sigmoid,
                              bias=col(bias + c)).then_inc(lora_out, 1)
                own(lora_out)
        for tb in range(TB):
            ac.wait_ge(vt_ps, tb + 1)
            ac.activation(vt[:, tb, :], banks[:, 6, :], ACT.Copy).then_inc(vt_done, 1)
            own(vt_done)
        ac.wait_ge(s_pback, 1)
        ac.activation(sprob[:, :, :], banks[:, 7, 0:NSB * B * H].rearrange("p (t n) -> p t n", t=NSB), ACT.Copy)\
            .then_inc(s_prob, 1)
        own(s_prob)
        for c in range(CC):
            ac.wait_ge(kk_in, c + 1)
            if c >= 1:
                ac.wait_ge(kk_ps, c)
            ac.activation(tmp[:, 0, :], rw[:, J_KK + c, :], ACT.Square).then_inc(kk_sq, 1)
            own(kk_sq)
            ac.wait_ge(kk_cl, c + 1)
            ac.activation(tmp[:, 1, :], tmp[:, 1, :], ACT.Sqrt).then_inc(kk_rt, 1)
            own(kk_rt)
        ac.wait_ge(ga_done, 6)
        ac.activation(gath[:, :, 1, :], gath[:, :, 1, :], ACT.Exp, scale=-DEC).then_inc(ga_exp, 1)
        own(ga_exp)
        ac.wait_ge(ends_in, 4)
        ac.activation(ends[:, :, :], ends[:, :, :], ACT.Exp).then_inc(ends_done, 1)
        own(ends_done)
        ac.wait_ge(ga_ps, 1)
        ac.activation(sixr[:, :], banks[0:6 * B, 6, :], ACT.Copy).then_inc(ga_row, 1)
        own(ga_row)
        ac.wait_ge(s_sum, 1)
        ac.activation(mixa_hi[:, :, T:TC], banks[:, 7, 0:CC * B].rearrange("p (c b) -> p c b", c=CC), ACT.Copy)\
            .then_inc(s_mix_hi, 1)
        own(s_mix_hi)

        def decays(n):
            if n >= 1:
                ac.wait_ge(qb_done, 4 * n)
            for c in range(CC):
                k = c * TB + n
                for i, sign in enumerate((-DEC, DEC)):
                    ac.activation(edec[:, i, c, :], cum[:, c, n, :], ACT.Exp, scale=sign, bias=refs[:, i, k:k + 1])\
                        .then_inc(edec_done, 1)
                    own(edec_done)

        def x0_copy(n):
            for g in range(2):
                ac.wait_ge(x0_ps, 2 * n + g + 1)
                ac.activation(xx[:, 4 * g:4 * g + 4, 0, :], banks[:, 4 + g, :].rearrange("p (h s) -> p h s", h=4),
                              ACT.Copy).then_inc(x0_done, 1)
                own(x0_done)

        def r_copy(n):
            ac.wait_ge(r_ps, n + 1)
            ac.activation(nr[:, :, :], banks[:, 6:8, 0:AW // 2], ACT.Copy, scale=-1.0).then_inc(r_done, 1)
            own(r_done)

        def u_copy(n):
            ac.wait_ge(u_ps, n + 1)
            ac.activation(uu[:, :], banks[:, 6, :], ACT.Copy).then_inc(u_done, 1)
            own(u_done)

        def y_copy(n):
            ac.wait_ge(y_ps, n + 1)
            ac.activation(yy[:, :, n * P:n * P + P], banks[:, 7, :].rearrange("p (c t) -> p c t", c=CC), ACT.Copy)\
                .then_inc(y_done, 1)
            own(y_done)

        ac.wait_ge(s_mix_lo, 1)
        decays(0)
        x0_copy(0)
        for c in range(CC):
            ac.activation(rw[:, J_V + c, :], rw[:, J_V + c, :], ACT.Identity, bias=col(C_GB + c)).then_inc(vb_done, 1)
            own(vb_done)
        for n in range(TB):
            if n >= 1:
                r_copy(n - 1)
            if n + 1 < TB:
                decays(n + 1)
            if n >= 1:
                u_copy(n - 1)
                y_copy(n - 1)
            for i in range(2):
                ac.wait_ge(bt_ps, 2 * n + i + 1)
                ac.activation(btok[:, i, :], banks[:, 6 + i, :], ACT.Copy).then_inc(bt_done, 1)
                own(bt_done)
            if n + 1 < TB:
                x0_copy(n + 1)
        ac.wait_ge(y_rows_ps, 1)
        ac.activation(yy[:, :, T + 1:XC:2], banks[:, 4, 0:CC * B].rearrange("p (c b) -> p c b", c=CC), ACT.Copy)\
            .then_inc(y_dec, 1)
        own(y_dec)
        for f in (r_copy, u_copy, y_copy):
            f(TB - 1)

        def gn_square(c):
            ac.wait_ge(gn_c, c + 1)
            if c >= 2:
                ac.wait_ge(gn_v, c - 1)
            ac.activation(sq[:, c % 2, :], yy[:, c, :], ACT.Square).then_inc(gn_q, 1)
            own(gn_q)

        def gn_root(c):
            ac.wait_ge(gn_v, c + 1)
            ac.activation(sd[:, c % 2, :].rearrange("p (a b) -> p a b", a=2), banks[:, 6:8, 0:XH], ACT.Sqrt,
                          bias=col(C_EPS + 1)).then_inc(gn_r, 1)
            own(gn_r)

        def gn_high(c):
            ac.wait_ge(gn_o, c + 1)
            ac.activation(mixb_hi[:, c, 0:T], yy[:, c, 0:T], ACT.Copy).then_inc(gn_hi, 1)
            own(gn_hi)
            ac.activation(mixb_hi[:, c, T:TC], yy[:, c, T + 1:XC:2], ACT.Copy).then_inc(gn_hi, 1)
            own(gn_hi)

        gn_square(0)
        gn_square(1)
        for c in range(CC):
            gn_root(c)
            if c >= 1:
                gn_high(c - 1)
            if c + 2 < CC:
                gn_square(c + 2)
        gn_high(CC - 1)
        w_high(N_IN)
        w_high(N_IN + 1)
        for s in range(N_IN + 2, S_FF + 2):
            w_high(s)

        def norm_act(k):
            for c in range(KT):
                n = k * KT + c
                ac.wait_ge(ln_c, n + 1)
                if n >= 2:
                    ac.wait_ge(ln_v, n - 1)
                ac.activation(lsq[:, c % 2, :], z[:, c, :], ACT.Square).then_inc(ln_q, 1)
                own(ln_q)
            ac.wait_ge(ln_v, KT * k + KT)
            ac.activation(lsd[:, :].rearrange("p (a b) -> p a b", a=2), banks[:, 6:8, 0:TH], ACT.Sqrt,
                          bias=col(C_EPS)).then_inc(ln_r, 1)
            own(ln_r)
            if k == 0:
                for c in range(KT):
                    ac.wait_ge(ln_o, c + 1)
                    ac.activation(x1_hi[:, c, :], z[:, c, :], ACT.Copy).then_inc(ln_hi, 1)
                    own(ln_hi)

        norm_act(0)
        for f in range(FT):
            o = S_FF + 2 * f
            w_high(o + 2)
            ac.wait_ge(slot_used, done(o))
            if f >= 2:
                ac.wait_ge(cv_ready, f - 1)
                ac.wait_ge(tail_done, f - 1)
            ac.activation(gp[:, f % 2, 2:2 + TC].rearrange("p (a b) -> p a b", a=2), bank2(o)[:, :, 0:TH], ACT.Copy)\
                .then_inc(gp_ready, 1)
            own(gp_ready)
            ac.wait_ge(cv_ready, f + 1)
            if f >= 1:
                ac.wait_ge(hh_ready, f)
            ac.activation(act[:, 0:T], cv[:, 0:T], ACT.Silu).then_inc(act_ready, 1)
            own(act_ready)
            ac.activation(act[:, T:TC], cv[:, T + 2 + B:T + 2 + B + 3 * B:3], ACT.Silu).then_inc(act_ready, 1)
            own(act_ready)
            w_high(o + 3)
            ac.wait_ge(hh_ready, f + 1)
            ac.activation(h_hi[:, f, :], hh[:, :], ACT.Copy).then_inc(h_hi_ready, 1)
            own(h_hi_ready)
        for s in range(S_DOWN + 2, N_SLOTS):
            w_high(s)
        norm_act(1)

    @block.vector
    def _(ve):
        own = settled(ve)
        chain = [0]

        def link(ins):
            chain[0] += 1
            ins.then_inc(dve, 1)
            ve.wait_ge(dve, chain[0])

        def tt(out, a0, a1, op):
            return ve.tensor_tensor(out, a0, a1, op)

        def stt(out, a0, s, a1, op0, op1):
            return ve.scalar_tensor_tensor(out, a0, s, a1, op0, op1)

        for k in range(KT):
            ve.wait_ge(x_hi_ready, k + 1)
            tt(x_lo[:, k, :], att[:, k, :], x_hi[:, k, :].bitcast(F32), ALU.subtract).then_inc(x_lo_ready, 1)
            own(x_lo_ready)
        ve.wait_ge(const_landed, 16 * 12)
        ve.wait_ge(pre_zero, 1)

        def shift(j):
            ve.wait_ge(in_copied, N_ATT + j + 1)
            cur, prev = pre[:, j % 2, 1:1 + XC], pre[:, j % 2, 0:XC]
            out = rw[:, j + CC * (j >= J_KK), :]
            link(tt(out, prev, cur, ALU.subtract))
            stt(out, out, col(C_MU + j), cur, ALU.mult, ALU.add).then_inc(rw_ready, 1)
            own(rw_ready)

        def soft(u):
            q, h = divmod(u, H)
            n = (q + 1) * P
            off = T - n
            if u >= 2:
                ve.wait_ge(a_probs_t, u - 1)
            link(stt(sw[:, u % 2, 0:n], dist[:, off:T], -slopes[h], lcount[:, off:T], ALU.mult, ALU.add))
            ve.wait_ge(a_scores, u + 1)
            stt(sw[:, u % 2, 0:n], banks[:, 4, 0:n], HD ** -0.5, sw[:, u % 2, 0:n], ALU.mult, ALU.add)\
                .then_inc(a_biased, 1)
            own(a_biased)
            ve.wait_ge(a_biased, u + 1)
            ve.tensor_reduce(nmax[:, u:u + 1], sw[:, u % 2, 0:n], AX, ALU.max, negate=True).then_inc(a_max, 1)
            own(a_max)

        def norm(q):
            ve.wait_ge(a_pv, H * (q + 1))
            link(ve.reciprocal(rinv[:, q * H:(q + 1) * H], rsum[:, q * H:(q + 1) * H]))
            if q >= 1:
                ve.wait_ge(a_back, q)
            tt(onrm[:, :].rearrange("p (h d) -> p h d", d=HD), banks[:, 6, :].rearrange("p (h d) -> p h d", d=HD),
               rinv[:, q * H:(q + 1) * H].unsqueeze(2).broadcast_to([P, H, HD]), ALU.mult).then_inc(a_norm, 1)
            own(a_norm)

        def mix_lo(q):
            ve.wait_ge(a_mix_hi, q + 1)
            tt(mixa_lo[:, :, q * P:q * P + P], banks[:, 6, :].rearrange("p (c t) -> p c t", c=CC),
               mixa_hi[:, :, q * P:q * P + P].bitcast(F32), ALU.subtract).then_inc(a_mix_lo, 1)
            own(a_mix_lo)

        def att_tick(k):
            if k < UNITS:
                soft(k)
            if k >= 2 and (k - 2) % H == H - 1:
                norm((k - 2) // H)
                mix_lo((k - 2) // H)

        def s_score(b):
            r = b % NKV
            ve.wait_ge(s_prod, b + 1)
            ve.tensor_reduce(sscore[:, :, b * H:(b + 1) * H],
                             kv[:, r, :].rearrange("p (t h d) -> p t h d", t=NSB, d=HD), AX, ALU.add)\
                .then_inc(s_red, 1)
            own(s_red)

        for s in range(N_ATT, N_IN + 1):
            if s >= N_ATT + 1:
                shift(s - 1 - N_ATT)
            for i, k in enumerate(ticks(s)):
                att_tick(k)
                if i == 0 and s > 0 and decode_row(s - 1) is not None:
                    s_score(decode_row(s - 1))
        ve.wait_ge(s_st, 1)
        link(stt(ssoft[:, :], banks[0:B * H, 7, 0:NSB * P], HD ** -0.5, sbias[:, :], ALU.mult, ALU.add))
        ve.tensor_reduce(sstat[:, 0:1], ssoft[:, :], AX, ALU.max, negate=True).then_inc(s_max, 1)
        own(s_max)
        ve.wait_ge(s_exp, 1)
        link(ve.reciprocal(sstat[:, 2:3], sstat[:, 1:2]))
        ve.tensor_scalar(ssoft[:, :], ssoft[:, :], sstat[:, 2:3], None, ALU.mult).then_inc(s_prn, 1)
        own(s_prn)

        def own_heads(g):
            ve.wait_ge(s_own_landed, 16)
            ve.wait_ge(s_pv, 4 * g + 4)
            tt(sw[:, g, :], banks[:, 7, :], pt[:, 0, :], ALU.mult).then_inc(s_own, 1)
            own(s_own)

        ve.wait_ge(slot_used, N_IN)
        ve.wait_ge(outs, 32)
        ve.tensor_copy(gath[:, :, 3, :], rw[:, J_V:J_V + CC, T + 1:XC:2]).then_inc(ga_done, 1)
        own(ga_done)
        link(ve.tensor_scalar(onemka[:, :], par[:, C_KA:C_KA + CC], -1.0, 1.0, ALU.mult, ALU.add))
        link(ve.memset(ones[:, :], 1.0))
        link(ve.memset(cum[:, :, :, 0:1], 0.0))
        for c in range(CC):
            r, k, v, kk = (rw[:, j + c, :] for j in (J_R, J_K, J_V, J_KK))
            ve.tensor_scalar(kk, k, col(C_KK + c), None, ALU.mult).then_inc(kk_in, 1)
            own(kk_in)
            ve.wait_ge(lora_out, 2 * c + 2)
            if c >= 1:
                ve.wait_ge(bo_ps, c)
            link(ve.tensor_scalar(tmp[:, 2, :], aa[:, c, :], col(C_KA + c), onemka[:, c:c + 1], ALU.mult, ALU.add))
            link(tt(k, k, tmp[:, 2, :], ALU.mult))
            stt(tmp[:, 2, :], r, col(C_RK + c), k, ALU.mult, ALU.mult).then_inc(bo_in, 1)
            own(bo_in)
            ve.wait_ge(kk_ps, c + 1)
            ve.tensor_scalar(tmp[:, 1, :].rearrange("p (a b) -> p a b", a=2), banks[:, 4:6, 0:XH], 1e-24, None,
                             ALU.max).then_inc(kk_cl, 1)
            own(kk_cl)
            for n in range(TB):
                link(ve.tensor_tensor_scan(cum[:, c, n, 1:P + 1], ones[:, :], yy[:, c, n * P:n * P + P], 0.0,
                                           ALU.mult, ALU.add))
            ve.wait_ge(kk_rt, c + 1)
            link(ve.reciprocal(tmp[:, 1, :], tmp[:, 1, :]))
            link(tt(kk, kk, tmp[:, 1, :], ALU.mult))
            tt(aa[:, c, :], kk, aa[:, c, :], ALU.mult).then_inc(kk_done, 1)
            own(kk_done)
            ve.wait_ge(bo_ps, c + 1)
            ve.wait_ge(vt_done, TB)
            tt(v.rearrange("p (a b) -> p a b", a=2), banks[:, 2 * (c % 2):2 * (c % 2) + 2, 0:XH],
               v.rearrange("p (a b) -> p a b", a=2), ALU.mult).then_inc(bo_done, 1)
            own(bo_done)
            if c % 2:
                own_heads(c // 2)
        for q, src in ((0, rw[:, J_R:J_R + CC]), (1, yy), (2, rw[:, J_K:J_K + CC]), (4, rw[:, J_KK:J_KK + CC]),
                       (5, aa)):
            ve.tensor_copy(gath[:, :, q, :], src[:, :, T + 1:XC:2]).then_inc(ga_done, 1)
            own(ga_done)
        mid = cum[:, :, :, 64]
        for i, sign in enumerate((DEC, -DEC)):
            ve.tensor_scalar(refs[:, i, :].rearrange("p (c n) -> p c n", c=CC), mid, sign, None, ALU.mult)\
                .then_inc(ends_in, 1)
            own(ends_in)
        ve.tensor_copy(ends[:, 0, :], refs[:, 1, :]).then_inc(ends_in, 1)
        own(ends_in)
        stt(ends[:, 1, :].rearrange("p (c n) -> p c n", c=CC), cum[:, :, :, P], -DEC,
            refs[:, 0, :].rearrange("p (c n) -> p c n", c=CC), ALU.mult, ALU.add).then_inc(ends_in, 1)
        own(ends_in)
        ve.wait_ge(s_mix_hi, 1)
        tt(mixa_lo[:, :, T:TC], banks[:, 7, 0:CC * B].rearrange("p (c b) -> p c b", c=CC),
           mixa_hi[:, :, T:TC].bitcast(F32), ALU.subtract).then_inc(s_mix_lo, 1)
        own(s_mix_lo)

        def transform(n):
            tok = slice(n * P, n * P + P)
            ve.wait_ge(edec_done, 8 * (n + 1))
            for x, e in ((rw[:, J_KK:J_KK + CC, tok], edec[:, 0, :, 0:P]),
                         (rw[:, J_R:J_R + CC, tok], edec[:, 0, :, 1:P + 1]),
                         (aa[:, :, tok], edec[:, 1, :, 1:P + 1]),
                         (rw[:, J_K:J_K + CC, tok], edec[:, 1, :, 1:P + 1])):
                tt(x, x, e, ALU.mult).then_inc(qb_done, 1)
                own(qb_done)

        def masked(n):
            for h in range(H):
                ve.wait_ge(sc_ps, H * n + h + 1)
                tt(ms[:, n % 2, h, :], banks[:, h % 4, :], causal[:, :], ALU.mult).then_inc(sc_done, 1)
                own(sc_done)
            for g in range(2):
                hs = slice(4 * g, 4 * g + 4)
                link(tt(pm[:, hs, :], ms[:, n % 2, hs, 0:P], level[:, 0, :].unsqueeze(1).broadcast_to([P, 4, P]),
                        ALU.mult))
                tt(xx[:, hs, 1, :], ident[:, :].unsqueeze(1).broadcast_to([P, 4, P]), pm[:, hs, :], ALU.subtract)\
                    .then_inc(xt_done, 1)
                own(xt_done)

        def by_tile(x):
            return x.rearrange("p (c v) -> p c v", c=CC)

        def per_tile(i, n):
            return ends[:, i, n::TB].unsqueeze(2).broadcast_to([P, CC, HD])

        def state_in(n):
            tt(by_tile(st[:, 1, :]), by_tile(st[:, 0, :]), per_tile(0, n), ALU.mult).then_inc(st_zero, 1)
            own(st_zero)

        def state_out(n):
            ve.wait_ge(st_ps, n + 1)
            link(tt(st[:, 1, :], st[:, 1, :], banks[:, 6, 0:CC * HD], ALU.add))
            tt(by_tile(st[:, 0, :]), by_tile(st[:, 1, :]), per_tile(1, n), ALU.mult).then_inc(st_done, 1)
            own(st_done)

        def halves(h0, n, l):
            for g in range(2):
                k = (NLEV - 1) * 2 * n + 2 * (l - 1) + g
                hs = slice(4 * g, 4 * g + 4)
                ve.wait_ge(p_ps, k + 1)
                if l < NLEV - 1:
                    tt(pm[:, hs, :], banks[:, 4 + g, :].rearrange("p (h s) -> p h s", h=4),
                       level[:, l, :].unsqueeze(1).broadcast_to([P, 4, P]), ALU.mult).then_inc(p_done, 1)
                    own(p_done)
                else:
                    ve.tensor_copy(pm[64:P, hs, 0:64], banks[64:P, 4 + g, 0:256].rearrange("p (h s) -> p h s", h=4))\
                        .then_inc(p_done, 1)
                    own(p_done)
            for g in range(2):
                k = (NLEV - 1) * 2 * n + 2 * (l - 1) + g
                hs = slice(4 * g, 4 * g + 4)
                ve.wait_ge(d_ps, k + 1)
                d = banks[:, 2 * g:2 * g + 2, :].rearrange("p a (i j s) -> p (a i) j s", i=2, j=2)
                if l < NLEV - 2:
                    tt(xx[:, hs, :, :].rearrange("p h a s -> p (h a s)"),
                       xx[:, hs, :, :].rearrange("p h a s -> p (h a s)"),
                       banks[:, 2 * g:2 * g + 2, :].rearrange("p a b -> p (a b)"), ALU.subtract).then_inc(d_done, 1)
                    own(d_done)
                elif l == NLEV - 2:
                    link(tt(xx[:, hs, 0, :], xx[:, hs, 0, :], d[:, :, 0, :], ALU.subtract))
                    tt(xf[:, hs, :], xx[:, hs, 1, :], d[:, :, 1, :], ALU.subtract).then_inc(d_done, 1)
                    own(d_done)
                else:
                    ve.tensor_scalar(xf[0:64, hs, 64:P], banks[0:64, 2 * g, 0:256].rearrange("p (h s) -> p h s", h=4),
                                     -1.0, None, ALU.mult).then_inc(d_done, 1)
                    own(d_done)

        ve.wait_ge(ends_done, 1)
        link(ve.memset(st[:, 0, :], 0.0))
        ve.memset(yy[:, :, T:XC:2], 0.0).then_inc(y_pad, 1)
        own(y_pad)
        transform(0)
        masked(0)
        state_in(0)
        for n in range(TB):
            for l in range(1, NLEV):
                halves(0, n, l)
                if n == 0 and l == 1:
                    ve.wait_ge(sw_a, 1)
                    ve.tensor_reduce(ssa[:, 0, :], swt[:, :, :], AX, ALU.add).then_inc(sw_sa, 1)
                    own(sw_sa)
                if n == 2 and l == 1:
                    ve.wait_ge(sw_a, 7)
                    ve.tensor_reduce(ssa[:, 1, :], swt[:, :, :], AX, ALU.add).then_inc(sw_y, 1)
                    own(sw_y)
                if l == 3 and n + 1 < TB:
                    transform(n + 1)
                if l == 4 and n >= 1:
                    state_out(n - 1)
                    state_in(n)
            if n + 1 < TB:
                masked(n + 1)
        state_out(TB - 1)

        def gn_center(c):
            ve.wait_ge(gn_m, c + 1)
            y2 = yy[:, c, :].rearrange("p (a b) -> p a b", a=2)
            tt(y2, y2, banks[:, 4:6, 0:XH], ALU.subtract).then_inc(gn_c, 1)
            own(gn_c)

        def gn_scale(c):
            ve.wait_ge(gn_r, c + 1)
            link(ve.reciprocal(rsd[:, :], sd[:, c % 2, :]))
            link(tt(yy[:, c, :], yy[:, c, :], rsd[:, :], ALU.mult))
            link(stt(yy[:, c, :], yy[:, c, :], col(C_GW + c), rw[:, J_V + c, :], ALU.mult, ALU.add))
            ve.wait_ge(gate_ps, c + 1)
            y2 = yy[:, c, :].rearrange("p (a b) -> p a b", a=2)
            tt(y2, y2, bank2(c)[:, :, 0:XH], ALU.mult).then_inc(gn_o, 1)
            own(gn_o)

        def gn_low(c):
            ve.wait_ge(gn_hi, 2 * c + 2)
            link(tt(mixb_lo[:, c, 0:T], yy[:, c, 0:T], mixb_hi[:, c, 0:T].bitcast(F32), ALU.subtract))
            tt(mixb_lo[:, c, T:TC], yy[:, c, T + 1:XC:2], mixb_hi[:, c, T:TC].bitcast(F32), ALU.subtract)\
                .then_inc(gn_lo, 1)
            own(gn_lo)

        gn_center(0)
        for c in range(CC):
            if c + 1 < CC:
                gn_center(c + 1)
            gn_scale(c)
            if c >= 1:
                gn_low(c - 1)
        gn_low(CC - 1)
        ve.wait_ge(z_landed, 32)

        def residual(k, o, c):
            ve.wait_ge(slot_used, done(o))
            z2 = z[:, c, :].rearrange("p (a b) -> p a b", a=2)
            stt(z2, z2, ALPHA, bank2(o)[:, :, 0:TH], ALU.mult, ALU.add).then_inc(z_ready, 1)
            own(z_ready)

        def norm_dve(k):
            ve.wait_ge(ln_m, k + 1)
            for c in range(KT):
                z2 = z[:, c, :].rearrange("p (a b) -> p a b", a=2)
                tt(z2, z2, banks[:, 4:6, 0:TH], ALU.subtract).then_inc(ln_c, 1)
                own(ln_c)
            ve.wait_ge(ln_r, k + 1)
            link(ve.reciprocal(lrs[:, :], lsd[:, :]))
            g, b = (C_L1G, C_L1B) if k == 0 else (C_L2G, C_L2B)

            def odd_low(c):
                ve.wait_ge(ln_hi, c + 1)
                tt(x1_lo[:, c, :], z[:, c, :], x1_hi[:, c, :].bitcast(F32), ALU.subtract).then_inc(ln_lo_odd, 1)
                own(ln_lo_odd)

            for c in range(KT):
                link(tt(z[:, c, :], z[:, c, :], lrs[:, :], ALU.mult))
                ve.tensor_scalar(z[:, c, :], z[:, c, :], col(g + c), col(b + c), ALU.mult, ALU.add).then_inc(ln_o, 1)
                own(ln_o)
                if k == 0 and c >= 2 and c % 2 == 0:
                    odd_low(c - 1)
            if k == 0:
                odd_low(KT - 1)

        for c in range(KT):
            residual(0, S_OUT + c, c)
        norm_dve(0)
        link(ve.memset(gp[:, :, 0:2], 0.0))
        for f in range(FT):
            o = S_FF + 2 * f
            base = T + 2 + B
            g = gp[:, f % 2, :]
            ve.wait_ge(gp_ready, f + 1)
            if f >= 1:
                ve.wait_ge(act_ready, 2 * f)
            tri = gp[:, f % 2, base:GW].rearrange("p (b e) -> p b e", e=3)
            link(ve.tensor_copy(tri[:, :, 0:2], cstate[:, f, :].rearrange("p (b e) -> p b e", e=2)))
            link(ve.tensor_copy(tri[:, :, 2:3], g[:, 2 + T:2 + TC].unsqueeze(2)))
            n = GW - 2
            ve.tensor_copy(tail[:, f, :], g[:, T:GW]).then_inc(tail_done, 1)
            own(tail_done)
            link(ve.tensor_scalar(cv[:, 0:n], g[:, 2:GW], col(C_CW + 2 * FT + f), col(C_CB + f), ALU.mult, ALU.add))
            link(stt(cv[:, 0:n], g[:, 1:GW - 1], col(C_CW + FT + f), cv[:, 0:n], ALU.mult, ALU.add))
            stt(cv[:, 0:n], g[:, 0:n], col(C_CW + f), cv[:, 0:n], ALU.mult, ALU.add).then_inc(cv_ready, 1)
            own(cv_ready)
            ve.wait_ge(act_ready, 2 * f + 2)
            ve.wait_ge(slot_used, done(o + 1))
            tt(hh[:, :].rearrange("p (a b) -> p a b", a=2), act[:, :].rearrange("p (a b) -> p a b", a=2),
               bank2(o + 1)[:, :, 0:TH], ALU.mult).then_inc(hh_ready, 1)
            own(hh_ready)
            ve.wait_ge(h_hi_ready, f + 1)
            tt(h_lo[:, f, :], hh[:, :], h_hi[:, f, :].bitcast(F32), ALU.subtract).then_inc(h_lo_ready, 1)
            own(h_lo_ready)
        for c in range(KT):
            residual(1, S_DOWN + c, c)
        norm_dve(1)

    @block.tensor
    def _(pe):
        def product(s, hi, lo, width, free, beside=None):
            o, k0, n, first, last = plan[s]
            pe.wait_ge(w_lo_ready, s + 1)
            if first:
                free(o)
            for i in range(n):
                wh, wl = (w[:, s % 2, i * P:(i + 1) * P] for w in (w_hi, w_lo))
                xh, xl = hi(k0 + i), lo(k0 + i)
                for t, (w, x) in enumerate(((wh, xh), (wh, xl), (wl, xh))):
                    for half in range(2):
                        ins = pe.matmul(bank2(o)[:, half, 0:width], w, x[:, half * width:(half + 1) * width],
                                        start=first and i == 0 and t == 0,
                                        stop=last and i == n - 1 and t == 2)
                if beside and i < n - 1:
                    beside(i)
            ins.then_inc(slot_used, 1)

        def mm(out, l, r, start=True, stop=True):
            return pe.matmul(out, l, r, start=start, stop=stop)

        def tok_rows():
            pe.wait_ge(const_landed, 16 * 12)
            pe.wait_ge(in_copied, N_ATT)
            for tb in range(TB):
                if tb >= 1:
                    pe.wait_ge(v_tok, tb)
                for c in range(CC):
                    ins = pe.transpose(banks[:, 5, c * P:(c + 1) * P], att[:, 2 * CC + c, tb * P:tb * P + P],
                                       ident[:, :])
                ins.then_inc(v_tok_ps, 1)
            for i in range(3):
                if i >= 1:
                    pe.wait_ge(s_rows, i)
                for c in range(CC):
                    ins = pe.transpose(banks[0:B, 7, c * P:(c + 1) * P], att[:, i * CC + c, T + 1:XC:2], ident[:, :])
                ins.then_inc(s_rows_ps, 1)

        def scores(u):
            q, h = divmod(u, H)
            lo, n = 64 * (h % 2), (q + 1) * P
            if u >= 1:
                pe.wait_ge(a_biased, u)
            mm(banks[:, 4, 0:n], att[lo:lo + 64, h // 2, q * P:q * P + P], att[lo:lo + 64, CC + h // 2, 0:n])\
                .then_inc(a_scores, 1)

        def probs_t(u):
            pe.wait_ge(a_exp, u + 1)
            if u == 0:
                pe.wait_ge(v_tok, TB)
            else:
                pe.wait_ge(a_pt, u)
            for j in range(u // H + 1):
                ins = pe.transpose(banks[:, 5, j * P:(j + 1) * P], sw[:, u % 2, j * P:(j + 1) * P], ident[:, :])
            ins.then_inc(a_probs_t, 1)

        def values(u):
            q, h = divmod(u, H)
            pe.wait_ge(a_pt, u + 1)
            if h == 0 and q >= 1:
                pe.wait_ge(a_mix_hi, q)
                pe.wait_ge(a_mix_lo, q)
            for j in range(q + 1):
                ins = mm(banks[:, 6, h * HD:(h + 1) * HD], pt[:, u % 2, j * P:(j + 1) * P],
                         vtok[:, j, h * HD:(h + 1) * HD], j == 0, j == q)
            ins.then_inc(a_pv, 1)

        def back(q):
            pe.wait_ge(a_norm, q + 1)
            for c in range(CC):
                ins = pe.transpose(banks[:, 6, c * P:(c + 1) * P], onrm[:, c * P:(c + 1) * P], ident[:, :])
            ins.then_inc(a_back, 1)

        def att_tick(k):
            if k < UNITS:
                scores(k)
            if 1 <= k <= UNITS:
                probs_t(k - 1)
            if k >= 2:
                values(k - 2)
                if (k - 2) % H == H - 1:
                    back((k - 2) // H)

        def spread_query(b):
            pe.wait_ge(s_rows, 3)
            if b >= 1:
                pe.wait_ge(s_qs, b)
            mm(banks[:, 7, :], ident[0:B, b:b + 1].broadcast_to([B, P]), srow[:, 0:AW]).then_inc(s_qb, 1)

        def x_part(k):
            pe.wait_ge(x_lo_ready, k + 1)
            return x_hi[:, k, :]

        for s in range(N_IN):
            steps = list(ticks(s))

            def beside(i):
                if i in (0, 3, 6) and i // 3 < len(steps):
                    att_tick(steps[i // 3])
                if i == 1 and decode_row(s) is not None:
                    spread_query(decode_row(s))

            product(s, x_part if s == 0 else lambda k: x_hi[:, k, :], lambda k: x_lo[:, k, :], XH,
                    lambda o: pe.wait_ge(in_copied, o - 1) if o >= 2 else None, beside)
            if s == FIRST_TICK - 1:
                tok_rows()
        pe.wait_ge(s_red, B)
        for t in range(NSB):
            ins = pe.transpose(banks[0:B * H, 7, t * P:(t + 1) * P], sscore[:, t, :], ident[:, :])
        ins.then_inc(s_st, 1)
        pe.wait_ge(lo_act, 2)
        pe.wait_ge(in_copied, N_IN)
        for c in range(CC):
            for i in range(2):
                g = 2 * c + i
                if g >= 2:
                    pe.wait_ge(lora_out, g - 1)
                for half in range(2):
                    ins = mm(bank2(g)[:, half, 0:XH], low_up[64 * i:64 * i + 64, c * P:(c + 1) * P],
                             rw[64 * i:64 * i + 64, J_WA, half * XH:(half + 1) * XH])
                ins.then_inc(lora_ps, 1)
        pe.wait_ge(rw_ready, N_RW)
        for tb in range(TB):
            if tb >= 1:
                pe.wait_ge(vt_done, tb)
            for c in range(CC):
                ins = pe.transpose(banks[:, 6, c * P:(c + 1) * P], rw[:, J_V + c, tb * P:tb * P + P], ident[:, :])
            ins.then_inc(vt_ps, 1)
        def decode_values(b):
            i, j = B + b, b % 4
            pe.wait_ge(s_prob, 1)
            pe.wait_ge(kv_landed[i % NKV], 64 * (i // NKV + 1))
            if b == 4:
                pe.wait_ge(s_own, 1)
            for t in range(NSB):
                ins = mm(banks[32 * j:32 * j + 32, 7, :], sprob[:, t, 32 * (b // 4):32 * (b // 4) + 32],
                         kv[:, i % NKV, t * AW:(t + 1) * AW], t == 0, t == NSB - 1)
            ins.then_inc(s_pv, 1)

        pe.wait_ge(lora_out, 2 * CC)
        pe.wait_ge(s_prn, 1)
        for t in range(NSB):
            ins = pe.transpose(banks[:, 7, t * B * H:(t + 1) * B * H], ssoft[:, t * P:(t + 1) * P],
                               ident[0:B * H, 0:B * H])
        ins.then_inc(s_pback, 1)
        for c in range(CC):
            pe.wait_ge(kk_sq, c + 1)
            if c >= 1:
                pe.wait_ge(kk_cl, c)
            for half in range(2):
                ins = mm(banks[:, 4 + half, 0:XH], head_sum[:, :], tmp[:, 0, half * XH:(half + 1) * XH])
            ins.then_inc(kk_ps, 1)
            pe.wait_ge(bo_in, c + 1)
            if c >= 2:
                pe.wait_ge(bo_done, c - 1)
            for half in range(2):
                ins = mm(banks[:, 2 * (c % 2) + half, 0:XH], head_sum[:, :], tmp[:, 2, half * XH:(half + 1) * XH])
            ins.then_inc(bo_ps, 1)
            decode_values(2 * c)
            decode_values(2 * c + 1)
        pe.wait_ge(ga_done, 6)
        pe.wait_ge(ga_exp, 1)
        for c in range(CC):
            ins = pe.transpose(banks[0:6 * B, 6, c * P:(c + 1) * P], gath[:, c, :, :].rearrange("p q b -> p (q b)"),
                               ident[:, :])
        ins.then_inc(ga_ps, 1)
        pe.wait_ge(s_own, 2)
        for g in range(2):
            for c in range(CC):
                ins = mm(banks[:, 7, c * B + 4 * g:c * B + 4 * g + 4], sw[:, g, c * P:(c + 1) * P],
                         par[:, C_QUAD:C_QUAD + 4])
        ins.then_inc(s_sum, 1)
        def head(h):
            return 64 * (h % 2), h // 2, slice(h * HD, (h + 1) * HD)

        def chunk_scores(n):
            pe.wait_ge(qb_done, 4 * n + 4)
            pe.wait_ge(bo_done, CC)
            if n >= 1:
                pe.wait_ge(d_done, 2 * (NLEV - 1) * n)
            tok = slice(n * P, n * P + P)
            for h in range(H):
                lo, c, _ = head(h)
                if h >= 4:
                    pe.wait_ge(sc_done, H * n + h - 3)
                for i, w in enumerate((aa[lo:lo + 64, c, tok], rw[lo:lo + 64, J_K + c, tok])):
                    ins = mm(banks[:, h % 4, 2 * P * i:2 * P * (i + 1)].rearrange("p (a t) -> p a t", a=2), w,
                             rw[lo:lo + 64, J_KK + c:J_R + c + 1:CC, tok])
                ins.then_inc(sc_ps, 1)
            for g in range(2):
                pe.wait_ge(xt_done, 2 * n + g + 1)
                for i in range(4):
                    ins = pe.transpose(banks[:, 4 + g, i * P:(i + 1) * P], xx[:, 4 * g + i, 1, :], ident[:, :])
                ins.then_inc(x0_ps, 1)

        def one_level(n, l):
            last = l == NLEV - 1
            for g in range(2):
                k = (NLEV - 1) * 2 * n + 2 * (l - 1) + g
                if l == 1:
                    pe.wait_ge(x0_done, 2 * n + g + 1)
                else:
                    pe.wait_ge(d_done, k - 1)
                for i in range(4):
                    h = 4 * g + i
                    if last:
                        ins = mm(banks[64:P, 4 + g, i * 64:(i + 1) * 64], ms[0:64, n % 2, h, 64:P], xx[0:64, h, 0, 0:64])
                    else:
                        ins = mm(banks[:, 4 + g, i * P:(i + 1) * P], ms[:, n % 2, h, 0:P], xx[:, h, 0, :])
                ins.then_inc(p_ps, 1)
            for g in range(2):
                k = (NLEV - 1) * 2 * n + 2 * (l - 1) + g
                pe.wait_ge(p_done, k + 1)
                for i in range(4):
                    h = 4 * g + i
                    if last:
                        ins = mm(banks[0:64, 2 * g, i * 64:(i + 1) * 64], pm[64:P, h, 0:64], xf[64:P, h, 64:P])
                    else:
                        o = banks[:, 2 * g + i // 2, 256 * (i % 2):256 * (i % 2) + 256]
                        mm(o[:, 0:P], xx[:, h, 1, :], pm[:, h, :])
                        ins = mm(o[:, P:2 * P], pm[:, h, :], xx[:, h, 1, :])
                ins.then_inc(d_ps, 1)

        def right_side(n):
            pe.wait_ge(st_zero, n + 1)
            pe.wait_ge(bt_done, 2 * n + 2)
            tok = slice(n * P, n * P + P)
            for h in range(H):
                lo, c, hc = head(h)
                o = banks[:, 6 + h % 2, c * HD:(c + 1) * HD]
                mm(o, rw[lo:lo + 64, J_KK + c, tok], st[lo:lo + 64, 1, c * HD:(c + 1) * HD], True, False)
                ins = mm(o, ms[:, n % 2, h, 2 * P:3 * P], vt[:, n, hc], False, True)
            ins.then_inc(r_ps, 1)

        def solve(n):
            pe.wait_ge(r_done, n + 1)
            pe.wait_ge(d_done, 2 * (NLEV - 1) * (n + 1))
            for h in range(H):
                ins = mm(banks[:, 6, h * HD:(h + 1) * HD], xf[:, h, :], nr[:, h % 2, h // 2 * HD:(h // 2 + 1) * HD])
            ins.then_inc(u_ps, 1)

        def outputs(n):
            pe.wait_ge(u_done, n + 1)
            tok = slice(n * P, n * P + P)
            for h in range(H):
                lo, c, hc = head(h)
                o = banks[lo:lo + 64, 7, c * P:(c + 1) * P]
                mm(o, st[lo:lo + 64, 1, c * HD:(c + 1) * HD], rw[lo:lo + 64, J_R + c, tok], True, False)
                mm(o, uu[:, hc], ms[:, n % 2, h, P:2 * P], False, False)
                ins = mm(o, vt[:, n, hc], ms[:, n % 2, h, 3 * P:4 * P], False, True)
            ins.then_inc(y_ps, 1)

        def state(n):
            pe.wait_ge(u_done, n + 1)
            for h in range(H):
                lo, c, hc = head(h)
                o = banks[lo:lo + 64, 6, c * HD:(c + 1) * HD]
                mm(o, btok[:, 0, hc], uu[:, hc], True, False)
                ins = mm(o, btok[:, 1, hc], vt[:, n, hc], False, True)
            ins.then_inc(st_ps, 1)

        def to_tokens(n):
            if n >= 1:
                pe.wait_ge(y_done, n)
                pe.wait_ge(st_done, n)
            else:
                pe.wait_ge(ga_row, 1)
                pe.wait_ge(s_mix_lo, 1)
            for i in range(2):
                for c in range(CC):
                    x = aa[:, c, n * P:n * P + P] if i == 0 else rw[:, J_K + c, n * P:n * P + P]
                    ins = pe.transpose(banks[:, 6 + i, c * P:(c + 1) * P], x, ident[:, :])
                ins.then_inc(bt_ps, 1)

        chunk_scores(0)
        for n in range(TB):
            for l in range(1, NLEV):
                one_level(n, l)
                if n >= 1 and l <= 4:
                    (right_side, solve, outputs, state)[l - 1](n - 1)
                if l == 5:
                    to_tokens(n)
            if n + 1 < TB:
                chunk_scores(n + 1)
        pe.wait_ge(y_landed, 32)
        pe.wait_ge(d_done, 2 * (NLEV - 1) * TB)
        for c in range(CC):
            ins = pe.transpose(banks[:, 4, c * B:(c + 1) * B], yrow[:, c * P:(c + 1) * P], ident[0:B, 0:B])
        ins.then_inc(y_rows_ps, 1)
        for f in (right_side, solve, outputs, state):
            f(TB - 1)
        pe.wait_ge(y_pad, 1)
        pe.wait_ge(y_done, TB)
        pe.wait_ge(y_dec, 1)
        pe.wait_ge(st_done, TB)

        def gn_mean(c):
            if c >= 1:
                pe.wait_ge(gn_c, c)
            for half in range(2):
                ins = mm(banks[:, 4 + half, 0:XH], head_mean[:, :], yy[:, c, half * XH:(half + 1) * XH])
            ins.then_inc(gn_m, 1)

        def gn_var(c):
            pe.wait_ge(gn_q, c + 1)
            if c >= 1:
                pe.wait_ge(gn_r, c)
            for half in range(2):
                ins = mm(banks[:, 6 + half, 0:XH], head_mean[:, :], sq[:, c % 2, half * XH:(half + 1) * XH])
            ins.then_inc(gn_v, 1)

        def gate(c):
            if c >= 2:
                pe.wait_ge(gn_o, c - 1)
            for half in range(2):
                o, hs = bank2(c)[:, half, 0:XH], slice(half * XH, (half + 1) * XH)
                mm(o, gate_up[:, 0, c * P:(c + 1) * P], rw[:, J_G, hs], True, False)
                ins = mm(o, gate_up[:, 1, c * P:(c + 1) * P], rw[:, J_G + 1, hs], False, True)
            ins.then_inc(gate_ps, 1)

        gn_mean(0)
        gn_mean(1)
        gate(0)
        gate(1)
        for c in range(CC):
            gn_var(c)
            if c + 2 < CC:
                gn_mean(c + 2)
                gate(c + 2)

        def means(c, n):
            pe.wait_ge(z_ready, n)
            for half in range(2):
                ins = mm(banks[:, 4 + half, 0:TH], all_mean[:, :], z[:, c, half * TH:(half + 1) * TH],
                         c == 0, c == KT - 1)
            if c == KT - 1:
                ins.then_inc(ln_m, 1)

        def variances(k):
            for c in range(KT):
                pe.wait_ge(ln_q, KT * k + c + 1)
                for half in range(2):
                    ins = mm(banks[:, 6 + half, 0:TH], all_mean[:, :], lsq[:, c % 2, half * TH:(half + 1) * TH],
                             c == 0, c == KT - 1)
                ins.then_inc(ln_v, 1)

        def mixed_hi(k):
            if k >= CC:
                pe.wait_ge(gn_lo, k - CC + 1)
            return mixa_hi[:, k, :] if k < CC else mixb_hi[:, k - CC, :]

        for c in range(KT):
            product(S_OUT + c, mixed_hi,
                    lambda k: mixa_lo[:, k, :] if k < CC else mixb_lo[:, k - CC, :], TH,
                    lambda o: pe.wait_ge(*((z_ready, o - S_OUT - 1) if o - S_OUT >= 2 else (gn_o, CC))))
            if c >= 1:
                means(c - 1, c)
        means(KT - 1, KT)
        variances(0)

        def x1_part(k):
            pe.wait_ge(ln_lo_odd if k % 2 else ln_lo_even, k // 2 + 1)
            return x1_hi[:, k, :]

        def ffn_free(o):
            f, up = divmod(o - S_FF, 2)
            if f == 0:
                pe.wait_ge(z_ready, KT)
            else:
                pe.wait_ge(hh_ready if up else gp_ready, f)

        for s in range(S_FF, S_DOWN):
            product(s, x1_part if s == S_FF else lambda k: x1_hi[:, k, :], lambda k: x1_lo[:, k, :], TH, ffn_free)

        def h_part(k):
            pe.wait_ge(h_lo_ready, k + 1)
            return h_hi[:, k, :]

        def down_free(o):
            m = o - S_DOWN
            if m < 2:
                pe.wait_ge(hh_ready, FT)
                pe.wait_ge(gp_ready, FT)
            else:
                pe.wait_ge(z_ready, KT + m - 1)

        for m in range(KT):
            for i in range(len(DOWN)):
                product(S_DOWN + len(DOWN) * m + i, h_part if m == 0 else lambda k: h_hi[:, k, :],
                        lambda k: h_lo[:, k, :], TH, down_free)
            if m >= 1:
                means(m - 1, KT + m)
        means(KT - 1, 2 * KT)
        variances(1)

    perm.close()


def weight_tiles(w):
    k, m = w.shape
    return w.reshape(k // P, P, m // P, P).transpose(2, 1, 0, 3).reshape(m // P, P, k)


def channel_major(x):
    return x.T.reshape(-1, P, x.shape[0]).transpose(1, 0, 2)


def kernel(**inputs):
    import concourse.bacc as bacc
    from concourse.bass_utils import run_bass_kernel_spmd

    v = {k: np.asarray(x) for k, x in inputs.items()}
    w = {k: x[0] for k, x in v.items() if k not in ("x_prompt", "x_sample")}
    xp, xs = v["x_prompt"][0], v["x_sample"][:, 0]

    pairs = np.stack([w["state_shift"], xs], 1).reshape(2 * B, D)
    w_in = np.concatenate([w["w_in"], np.zeros((D, -w["w_in"].shape[1] % P), np.float32)], 1)
    mu = np.concatenate([w["mu_shift"], np.zeros(-len(w["mu_shift"]) % P, np.float32)])
    w_ff = weight_tiles(w["w_ffn_in"]).reshape(2, FT, P, D).transpose(1, 0, 2, 3).reshape(2 * FT, P, D)
    down = weight_tiles(w["w_ffn_out"])
    slots = np.zeros((N_SLOTS, P, KT * P), np.float32)
    slots[:N_IN] = weight_tiles(w_in)[IN_ORDER]
    slots[S_OUT:S_FF] = weight_tiles(w["w_out"])
    slots[S_FF:S_DOWN] = w_ff
    for i, (k0, k1) in enumerate(DOWN):
        slots[S_DOWN + i::len(DOWN), :, :(k1 - k0) * P] = down[:, :, k0 * P:k1 * P]
    mu_tiles = mu.reshape(-1, P)[[m - N_ATT for m in IN_ORDER[N_ATT:]]]
    rows = [mu_tiles] + [w[n].reshape(-1, P) for n in
                         ("w0", "a0", "k_k", "k_a", "r_k", "gn_w", "gn_b", "ln1_g", "ln1_b", "ln2_g", "ln2_b",
                          "conv_w", "conv_b")]
    rows.append(np.array([[LN_EPS] * P, [GN_EPS] * P], np.float32))
    arrays = shape_constants()
    rows.append(arrays.pop("quad").T)
    arrays.update(
        x=channel_major(np.concatenate([xp, pairs])),
        xc=channel_major(np.concatenate([xp, xs])),
        x_last=np.concatenate([xp[-1:], xs]),
        w=slots,
        par=np.concatenate(rows).T,
        low_up=np.concatenate([w["w_lora_up"], w["a_lora_up"]]),
        gate_up=np.concatenate([w["g_lora_up"], np.zeros((2 * P - GL, AW), np.float32)]).reshape(2, P, AW)
        .transpose(1, 0, 2),
        ck=w["cache_k_win"], cv=w["cache_v_win"],
        swkv=w["state_wkv"].reshape(B * H, HD, HD),
        cstate=w["state_conv"].transpose(2, 0, 1).reshape(FT, P, 2 * B).transpose(1, 0, 2),
    )
    arrays = {k: np.ascontiguousarray(x) for k, x in arrays.items()}
    out_shapes = {
        "y_out": (P, KT, TC), "att_out": (P, 2 * CC, XC), "shift_out": (1 + B, D), "wkv_out": (P, CC * HD),
        "swkv_out": (B * H, HD, HD), "conv_out": (P, FT, 34),
    }
    nc = bacc.Bacc("TRN2", target_bir_lowering=False, num_devices=1)
    aps = {k: nc.dram_tensor(f"in_{k}", x.shape, F32, kind="ExternalInput").ap() for k, x in arrays.items()}
    for k, s in out_shapes.items():
        aps[k] = nc.dram_tensor(k, s, F32, kind="ExternalOutput").ap()
    layer(nc, aps)
    r = run_bass_kernel_spmd(nc, [{f"in_{k}": x for k, x in arrays.items()}], core_ids=[0]).results[0]

    def token_major(x):
        return x.transpose(2, 1, 0).reshape(x.shape[2], -1)

    y = token_major(r["y_out"])
    k_all, v_all = token_major(r["att_out"][:, :CC]), token_major(r["att_out"][:, CC:])
    new = slice(T + 1, XC, 2)
    wkv = r["wkv_out"].reshape(2, HD, CC, HD).transpose(2, 0, 3, 1).reshape(H, HD, HD)
    conv = r["conv_out"].transpose(2, 1, 0).reshape(34, FF)
    csample = conv[2 + B:].reshape(B, 3, FF)[:, 1:]
    return (y[None, :T], y[T:, None], k_all[:T].reshape(1, 1, T, H, HD), v_all[:T].reshape(1, 1, T, H, HD),
            k_all[new].reshape(1, B, 1, H, HD), v_all[new].reshape(1, B, 1, H, HD),
            r["shift_out"][None, :1], r["shift_out"][None, 1:], wkv[None, None],
            r["swkv_out"].reshape(1, B, H, HD, HD), conv[None, None, :2], csample[None])
```
